# Optimizing a Trainium2 kernel written in Bass

```python
import math
import jax, jax.numpy as jnp
from jax import lax
import numpy as np

D_MODEL = 2048
BATCH = 1
SEQ = 256
DEPTH = 1
DEC_BATCH = 8
DEC_SEQ = 8
PAST_LEN = 2048
PAGE_SIZE = 128

HEAD_DIM = 128
H_FOX = 8
DIL_PAIRS = ((128, 1), (512, 4), (2048, 16))
N_GROUPS = 3
H_PER_GROUP = 4
H_DIL = N_GROUPS * H_PER_GROUP
N_BUCKETS = 32
MAX_DISTANCE = 2048
D_FF = -(-(8 * D_MODEL) // (3 * 256)) * 256
D_FOX = H_FOX * HEAD_DIM
D_DIL = H_DIL * HEAD_DIM
D_DIL_OUT = H_PER_GROUP * HEAD_DIM
IN_SPLITS = (D_FOX, 2 * D_FOX, 3 * D_FOX, 3 * D_FOX + H_FOX, 3 * D_FOX + H_FOX + D_DIL, 3 * D_FOX + H_FOX + 2 * D_DIL)
D_IN = 3 * D_FOX + H_FOX + 3 * D_DIL
Q_BLOCK = 128
ATTN_SCALE = HEAD_DIM ** -0.5
RMS_EPS = 1e-6
NEG_INF = -1e30
FORGET_BIAS_INIT = 7.0

kernel_name = 'fox_dilated_hybrid_step'

def rmsnorm(x, g):
    xf = x.astype(jnp.float32)
    y = xf * lax.rsqrt(jnp.mean(xf * xf, axis=-1, keepdims=True) + RMS_EPS)
    return (y * g.astype(jnp.float32)).astype(x.dtype)

def t5_bucket(dist):
    max_exact = N_BUCKETS // 2
    d_f = jnp.maximum(dist, 1).astype(jnp.float32)
    large = max_exact + (jnp.log(d_f / max_exact) / math.log(MAX_DISTANCE / max_exact) * (N_BUCKETS - max_exact)).astype(jnp.int32)
    return jnp.where(dist < max_exact, dist, jnp.minimum(large, N_BUCKETS - 1))

def swiglu(h, w_gate_up, w_down):
    gu = jnp.einsum('bsd,df->bsf', h, w_gate_up)
    g, u = jnp.split(gu, 2, axis=-1)
    return jnp.einsum('bsf,fd->bsd', jax.nn.silu(g) * u, w_down)

def project_in(h, w_in, b_forget):
    B, S, _ = h.shape
    proj = jnp.einsum('bsd,de->bse', h, w_in)
    q_f, k_f, v_f, f_logit, q_d, k_d, v_d = jnp.split(proj, IN_SPLITS, axis=-1)
    fox = lambda t: t.reshape(B, S, H_FOX, HEAD_DIM)
    dil = lambda t: t.reshape(B, S, N_GROUPS, H_PER_GROUP, HEAD_DIM)
    log_f = jax.nn.log_sigmoid((f_logit + b_forget).astype(jnp.float32))
    return fox(q_f), fox(k_f), fox(v_f), log_f, dil(q_d), dil(k_d), dil(v_d)

def fox_attend(q, k, v, bias_q, bias_k, q_pos, k_pos):
    s = jnp.einsum('bqhd,bshd->bhqs', q, k).astype(jnp.float32) * ATTN_SCALE
    s = s + jnp.transpose(bias_q, (0, 2, 1))[:, :, :, None] + jnp.transpose(bias_k, (0, 2, 1))[:, :, None, :]
    causal = k_pos[None, :] <= q_pos[:, None]
    s = jnp.where(causal[None, None], s, NEG_INF)
    p = jax.nn.softmax(s, axis=-1)
    return jnp.einsum('bhqs,bshd->bqhd', p.astype(v.dtype), v)

def fox_prompt(q, k, v, log_f):
    B, S = q.shape[:2]
    n_blk = S // Q_BLOCK
    c = jnp.cumsum(log_f, axis=1)
    k_pos = jnp.arange(S, dtype=jnp.int32)
    q_blocks = q.reshape(B, n_blk, Q_BLOCK, H_FOX, HEAD_DIM).swapaxes(0, 1)
    c_blocks = c.reshape(B, n_blk, Q_BLOCK, H_FOX).swapaxes(0, 1)
    starts = jnp.arange(n_blk, dtype=jnp.int32) * Q_BLOCK

    def body(args):
        q_blk, c_blk, start = args
        q_pos = start + jnp.arange(Q_BLOCK, dtype=jnp.int32)
        return fox_attend(q_blk, k, v, c_blk, -c, q_pos, k_pos)

    o = lax.map(body, (q_blocks, c_blocks, starts))
    return o.swapaxes(0, 1).reshape(B, S, H_FOX, HEAD_DIM)

def fox_sample(q, k_new, v_new, log_f_new, cache_k, cache_v, cache_logf, page_table):
    B, T = q.shape[:2]
    past_k = cache_k[page_table].reshape(B, -1, H_FOX, HEAD_DIM)
    past_v = cache_v[page_table].reshape(B, -1, H_FOX, HEAD_DIM)
    past_lf = cache_logf[page_table].reshape(B, -1, H_FOX).astype(jnp.float32)
    P = past_k.shape[1]
    k_all = jnp.concatenate([past_k, k_new.astype(past_k.dtype)], axis=1)
    v_all = jnp.concatenate([past_v, v_new.astype(past_v.dtype)], axis=1)
    g_new = jnp.cumsum(log_f_new, axis=1)
    past_suffix = jnp.flip(jnp.cumsum(jnp.flip(past_lf, axis=1), axis=1), axis=1) - past_lf
    bias_k = jnp.concatenate([past_suffix, -g_new], axis=1)
    q_pos = P + jnp.arange(T, dtype=jnp.int32)
    k_pos = jnp.arange(P + T, dtype=jnp.int32)
    return fox_attend(q, k_all, v_all, g_new, bias_k, q_pos, k_pos)

def dilated_group_attend(q, k_all, v_all, q_idx, window, dil, table_g):
    n_steps = window // dil + 1
    steps = jnp.arange(n_steps, dtype=jnp.int32)
    idx = q_idx[:, None] - steps[None, :] * dil
    valid = idx >= 0
    idx_c = jnp.maximum(idx, 0)
    kg = k_all[:, idx_c]
    vg = v_all[:, idx_c]
    rel = table_g[t5_bucket(steps * dil)]
    s = jnp.einsum('bqhd,bqnhd->bhqn', q, kg).astype(jnp.float32) * ATTN_SCALE
    s = s + rel.astype(jnp.float32).T[None, :, None, :]
    s = jnp.where(valid[None, None], s, NEG_INF)
    lse = jax.nn.logsumexp(s, axis=-1)
    p = jnp.exp(s - lse[..., None])
    o = jnp.einsum('bhqn,bqnhd->bqhd', p.astype(vg.dtype), vg)
    return o, jnp.transpose(lse, (0, 2, 1))

def combine_groups(outs, lses):
    w = jax.nn.softmax(jnp.stack(lses, axis=0), axis=0)
    o = jnp.stack(outs, axis=0)
    return jnp.einsum('gbqh,gbqhd->bqhd', w.astype(o.dtype), o)

def group_tables(rel_bias_table):
    return [rel_bias_table[:, g * H_PER_GROUP:(g + 1) * H_PER_GROUP] for g in range(N_GROUPS)]

def dilated_prompt(q_d, k_d, v_d, rel_bias_table):
    B, S = q_d.shape[:2]
    n_blk = S // Q_BLOCK
    tables = group_tables(rel_bias_table)
    k_groups = [k_d[:, :, g] for g in range(N_GROUPS)]
    v_groups = [v_d[:, :, g] for g in range(N_GROUPS)]
    q_blocks = q_d.reshape(B, n_blk, Q_BLOCK, N_GROUPS, H_PER_GROUP, HEAD_DIM).swapaxes(0, 1)
    starts = jnp.arange(n_blk, dtype=jnp.int32) * Q_BLOCK

    def body(args):
        q_blk, start = args
        q_idx = start + jnp.arange(Q_BLOCK, dtype=jnp.int32)
        outs, lses = [], []
        for g, (window, dil) in enumerate(DIL_PAIRS):
            o, l = dilated_group_attend(q_blk[:, :, g], k_groups[g], v_groups[g], q_idx, window, dil, tables[g])
            outs.append(o)
            lses.append(l)
        return combine_groups(outs, lses)

    o = lax.map(body, (q_blocks, starts))
    return o.swapaxes(0, 1).reshape(B, S, H_PER_GROUP, HEAD_DIM)

def dilated_sample(q_d, k_alls, v_alls, buf_lens, rel_bias_table):
    T = q_d.shape[1]
    tables = group_tables(rel_bias_table)
    outs, lses = [], []
    for g, (window, dil) in enumerate(DIL_PAIRS):
        q_idx = buf_lens[g] + jnp.arange(T, dtype=jnp.int32)
        o, l = dilated_group_attend(q_d[:, :, g], k_alls[g], v_alls[g], q_idx, window, dil, tables[g])
        outs.append(o)
        lses.append(l)
    return combine_groups(outs, lses)

def merge_out(h, o_fox, o_dil, w_gate, b_gate, w_o_fox, w_o_dil, w_out):
    B, S, _ = h.shape
    gates = jax.nn.sigmoid(jnp.einsum('bsd,de->bse', h, w_gate) + b_gate)
    g_fox, g_dil = jnp.split(gates, 2, axis=-1)
    y_fox = jnp.einsum('bse,ed->bsd', o_fox.reshape(B, S, D_FOX), w_o_fox)
    y_dil = jnp.einsum('bse,ed->bsd', o_dil.reshape(B, S, D_DIL_OUT), w_o_dil)
    return jnp.einsum('bse,ed->bsd', g_fox * y_fox + g_dil * y_dil, w_out)

def mixer_prompt(h, rel_bias_table, w_in, b_forget, w_gate, b_gate, w_o_fox, w_o_dil, w_out):
    q_f, k_f, v_f, log_f, q_d, k_d, v_d = project_in(h, w_in, b_forget)
    o_fox = fox_prompt(q_f, k_f, v_f, log_f)
    o_dil = dilated_prompt(q_d, k_d, v_d, rel_bias_table)
    y = merge_out(h, o_fox, o_dil, w_gate, b_gate, w_o_fox, w_o_dil, w_out)
    S = h.shape[1]
    win_rows = []
    for g, (window, _) in enumerate(DIL_PAIRS):
        keep = min(window, S)
        win_rows.append(k_d[:, S - keep:, g])
        win_rows.append(v_d[:, S - keep:, g])
    return y, (k_f, v_f, log_f), win_rows

def mixer_sample(h, cache_k, cache_v, cache_logf, page_table, win_k, win_v, rel_bias_table,
                 w_in, b_forget, w_gate, b_gate, w_o_fox, w_o_dil, w_out):
    q_f, k_f, v_f, log_f, q_d, k_d, v_d = project_in(h, w_in, b_forget)
    o_fox = fox_sample(q_f, k_f, v_f, log_f, cache_k, cache_v, cache_logf, page_table)
    k_alls = [jnp.concatenate([win_k[g], k_d[:, :, g].astype(win_k[g].dtype)], axis=1) for g in range(N_GROUPS)]
    v_alls = [jnp.concatenate([win_v[g], v_d[:, :, g].astype(win_v[g].dtype)], axis=1) for g in range(N_GROUPS)]
    buf_lens = [win_k[g].shape[1] for g in range(N_GROUPS)]
    o_dil = dilated_sample(q_d, k_alls, v_alls, buf_lens, rel_bias_table)
    y = merge_out(h, o_fox, o_dil, w_gate, b_gate, w_o_fox, w_o_dil, w_out)
    win_rows = []
    for g in range(N_GROUPS):
        win_rows.append(k_alls[g][:, -buf_lens[g]:])
        win_rows.append(v_alls[g][:, -buf_lens[g]:])
    return y, (k_f, v_f, log_f), win_rows

def finish_layer(x, m, g_post_mix, g_pre_ffn, g_post_ffn, w_gate_up, w_down):
    x = x + rmsnorm(m, g_post_mix)
    return x + rmsnorm(swiglu(rmsnorm(x, g_pre_ffn), w_gate_up, w_down), g_post_ffn)

def stack_layers(rows, i):
    return jnp.stack([r[i] for r in rows], axis=0)

def setup_inputs(seed: int = 0) -> dict:
    key = jax.random.key(seed)
    ks = jax.random.split(key, 32)
    f32 = jnp.float32
    n_pages = PAST_LEN // PAGE_SIZE
    n_used = DEC_BATCH * n_pages
    n_phys = n_used + max(1, n_used // 4)

    def nrm(k, shape, scale):
        return jax.random.normal(k, shape, f32) * scale

    win_lens = [min(w, PAST_LEN) for (w, _) in DIL_PAIRS]
    page_table = jax.random.permutation(ks[5], n_phys)[:n_used].reshape(DEC_BATCH, n_pages).astype(jnp.int32)
    return {
        'x_prompt': nrm(ks[0], (BATCH, SEQ, D_MODEL), 1.0),
        'x_sample': nrm(ks[1], (DEC_BATCH, DEC_SEQ, D_MODEL), 1.0),
        'cache_fox_k': nrm(ks[2], (DEPTH, n_phys, PAGE_SIZE, H_FOX, HEAD_DIM), 1.0),
        'cache_fox_v': nrm(ks[3], (DEPTH, n_phys, PAGE_SIZE, H_FOX, HEAD_DIM), 1.0),
        'cache_fox_logf': jax.nn.log_sigmoid(FORGET_BIAS_INIT + nrm(ks[4], (DEPTH, n_phys, PAGE_SIZE, H_FOX), 1.0)),
        'page_table': page_table,
        'cache_win1_k': nrm(ks[6], (DEPTH, DEC_BATCH, win_lens[0], H_PER_GROUP, HEAD_DIM), 1.0),
        'cache_win1_v': nrm(ks[7], (DEPTH, DEC_BATCH, win_lens[0], H_PER_GROUP, HEAD_DIM), 1.0),
        'cache_win2_k': nrm(ks[8], (DEPTH, DEC_BATCH, win_lens[1], H_PER_GROUP, HEAD_DIM), 1.0),
        'cache_win2_v': nrm(ks[9], (DEPTH, DEC_BATCH, win_lens[1], H_PER_GROUP, HEAD_DIM), 1.0),
        'cache_win3_k': nrm(ks[10], (DEPTH, DEC_BATCH, win_lens[2], H_PER_GROUP, HEAD_DIM), 1.0),
        'cache_win3_v': nrm(ks[11], (DEPTH, DEC_BATCH, win_lens[2], H_PER_GROUP, HEAD_DIM), 1.0),
        'rel_bias_table': nrm(ks[12], (N_BUCKETS, H_DIL), 0.5),
        'norm_pre_mix': 1.0 + nrm(ks[13], (DEPTH, D_MODEL), 0.1),
        'norm_post_mix': 1.0 + nrm(ks[14], (DEPTH, D_MODEL), 0.1),
        'norm_pre_ffn': 1.0 + nrm(ks[15], (DEPTH, D_MODEL), 0.1),
        'norm_post_ffn': 1.0 + nrm(ks[16], (DEPTH, D_MODEL), 0.1),
        'w_in': nrm(ks[17], (DEPTH, D_MODEL, D_IN), D_MODEL ** -0.5),
        'b_forget': FORGET_BIAS_INIT + nrm(ks[18], (DEPTH, H_FOX), 0.5),
        'w_gate': nrm(ks[19], (DEPTH, D_MODEL, 2 * D_MODEL), D_MODEL ** -0.5),
        'b_gate': nrm(ks[20], (DEPTH, 2 * D_MODEL), 0.1),
        'w_o_fox': nrm(ks[21], (DEPTH, D_FOX, D_MODEL), D_FOX ** -0.5),
        'w_o_dil': nrm(ks[22], (DEPTH, D_DIL_OUT, D_MODEL), D_DIL_OUT ** -0.5),
        'w_out': nrm(ks[23], (DEPTH, D_MODEL, D_MODEL), D_MODEL ** -0.5),
        'w_gate_up': nrm(ks[24], (DEPTH, D_MODEL, 2 * D_FF), D_MODEL ** -0.5),
        'w_down': nrm(ks[25], (DEPTH, D_FF, D_MODEL), D_FF ** -0.5),
    }

def reference(x_prompt, x_sample, cache_fox_k, cache_fox_v, cache_fox_logf, page_table,
              cache_win1_k, cache_win1_v, cache_win2_k, cache_win2_v, cache_win3_k, cache_win3_v,
              rel_bias_table, norm_pre_mix, norm_post_mix, norm_pre_ffn, norm_post_ffn,
              w_in, b_forget, w_gate, b_gate, w_o_fox, w_o_dil, w_out, w_gate_up, w_down):
    xp, xs = x_prompt, x_sample
    fox_p_rows, fox_s_rows, win_p_rows, win_s_rows = [], [], [], []
    for l in range(DEPTH):
        mix_w = (w_in[l], b_forget[l], w_gate[l], b_gate[l], w_o_fox[l], w_o_dil[l], w_out[l])
        ffn_w = (norm_post_mix[l], norm_pre_ffn[l], norm_post_ffn[l], w_gate_up[l], w_down[l])
        m_p, fox_p, win_p = mixer_prompt(rmsnorm(xp, norm_pre_mix[l]), rel_bias_table, *mix_w)
        xp = finish_layer(xp, m_p, *ffn_w)
        m_s, fox_s, win_s = mixer_sample(
            rmsnorm(xs, norm_pre_mix[l]), cache_fox_k[l], cache_fox_v[l], cache_fox_logf[l], page_table,
            [cache_win1_k[l], cache_win2_k[l], cache_win3_k[l]],
            [cache_win1_v[l], cache_win2_v[l], cache_win3_v[l]],
            rel_bias_table, *mix_w)
        xs = finish_layer(xs, m_s, *ffn_w)
        fox_p_rows.append(fox_p)
        fox_s_rows.append(fox_s)
        win_p_rows.append(win_p)
        win_s_rows.append(win_s)
    return (xp, xs,
            stack_layers(fox_p_rows, 0), stack_layers(fox_p_rows, 1), stack_layers(fox_p_rows, 2),
            stack_layers(fox_s_rows, 0), stack_layers(fox_s_rows, 1), stack_layers(fox_s_rows, 2),
            stack_layers(win_p_rows, 0), stack_layers(win_p_rows, 1), stack_layers(win_p_rows, 2),
            stack_layers(win_p_rows, 3), stack_layers(win_p_rows, 4), stack_layers(win_p_rows, 5),
            stack_layers(win_s_rows, 0), stack_layers(win_s_rows, 1), stack_layers(win_s_rows, 2),
            stack_layers(win_s_rows, 3), stack_layers(win_s_rows, 4), stack_layers(win_s_rows, 5))


_drawn_inputs = setup_inputs


def setup_inputs(seed=0):
    import zlib

    import numpy as np

    out = dict(_drawn_inputs(seed))
    spreads = {}
    factors = {'cache_fox_logf': 6.176}
    for name, (base, spread) in spreads.items():
        noise = np.random.default_rng([zlib.crc32(name.encode()), seed]).standard_normal(out[name].shape)
        drawn = base * np.exp(spread * noise) if base else spread * noise
        out[name] = __import__('jax').numpy.asarray(drawn.astype(out[name].dtype))
    for name, factor in factors.items():
        out[name] = (out[name] * factor).astype(out[name].dtype)
    return out
```

```python
from contextlib import ExitStack

import numpy as np

import concourse.bass as bass
from concourse import mybir

F32 = mybir.dt.float32
F32R = mybir.dt.float32r
U32 = mybir.dt.uint32
I32 = mybir.dt.int32
ALU = mybir.AluOpType
ACT = mybir.ActivationFunctionType
AX = mybir.AxisListType.X

P = 128
DM = 2048
KT = DM // P
SEQ, DB, DT = 256, 8, 8
NS = DB * DT
T = SEQ + NS
HD = 128
HF, HG, NG = 8, 4, 3
HDIL = HG * NG
NB = 32
DFF = 5632
FB = DFF // P
KQ = 11
PAST, PAGE = 2048, 128
NPG = PAST // PAGE
DIL = ((128, 1), (512, 4), (2048, 16))
SCALE = HD ** -0.5
EPS = 1e-6
NEG = -1e30
NQ = HF + HDIL
KPG = NPG + 1 + 2 + 4

U_FQ, U_FK, U_FV = 0, 8, 16
U_DQ, U_DK, U_DV = 24, 36, 48
U_GATE = 60
U_O = U_GATE + 2 * KT
U_OUT = U_O + KT
U_UP = U_OUT + KT
U_DOWN = U_UP + 2 * FB
U_END = U_DOWN + 4 * KT

C_ID, C_REV, C_UP, C_LOW, C_CAUSAL, C_UPB, C_BLK, C_END = 0, 128, 256, 384, 512, 640, 704, 768


def t5_bucket(dist):
    exact = NB // 2
    d = np.maximum(dist, 1).astype(np.float32)
    large = exact + (np.log(d / np.float32(exact)) / np.float32(np.log(2048 / exact)) * (NB - exact)).astype(np.int32)
    return np.where(dist < exact, dist, np.minimum(large, NB - 1))


def shape_consts():
    c = np.zeros((P, C_END), np.float32)
    i, j = np.arange(P)[:, None], np.arange(P)[None, :]
    c[:, C_ID:C_ID + P] = i == j
    c[:, C_REV:C_REV + P] = i + j == P - 1
    c[:, C_UP:C_UP + P] = i <= j
    c[:, C_LOW:C_LOW + P] = i > j
    c[:, C_CAUSAL:C_CAUSAL + P] = np.where(j <= i, 0.0, NEG)
    a, b = np.arange(NS)[:, None], np.arange(NS)[None, :]
    same = a // DT == b // DT
    c[:NS, C_UPB:C_UPB + NS] = same & (a <= b)
    c[:NS, C_BLK:C_BLK + NS] = np.where(same & (a <= b), 0.0, NEG)
    return c


def bucket_picks():
    s = np.zeros((NB + 1, NG, DT, P + NS), np.float32)
    r = np.zeros((NB + 1, NG, 384), np.float32)
    for g, (window, dil) in enumerate(DIL):
        for q in range(DT):
            step = P + q // dil - np.arange(P)
            dist = step * dil
            ok = step <= window // dil
            bucket = np.where(ok, t5_bucket(dist), NB)
            s[bucket, g, q, np.arange(P)] = 1
            d = q - np.arange(NS) % DT
            ok = (d >= 0) & (d % dil == 0)
            s[np.where(ok, t5_bucket(np.maximum(d, 0)), NB), g, q, P + np.arange(NS)] = 1
        d = 255 - np.arange(384)
        ok = (d >= 0) & (d % dil == 0) & (d <= window)
        r[np.where(ok, t5_bucket(np.maximum(d, 0)), NB), g, np.arange(384)] = 1
    return np.concatenate([s.reshape(NB + 1, -1), r.reshape(NB + 1, -1)], 1)


SPICK = NG * DT * (P + NS)
NPICK = SPICK + NG * 384


class Tally:

    def __init__(self, sem):
        self.sem, self.base, self.k, self.reg = sem, 0, 0, None

    def inc(self, ins):
        ins.then_inc(self.sem, 1)
        self.k += 1

    def value(self):
        return self.base + self.k if self.reg is None else self.reg + (self.base + self.k)

    def wait(self, eng):
        eng.wait_ge(self.sem, self.value())

    def enter(self, i, per):
        self.base += self.k
        self.k, self.reg, self.per = 0, i * per, per

    def leave(self, trips):
        assert self.k == self.per, (self.k, self.per)
        self.base += trips * self.per
        self.k, self.reg = 0, None


def build(nc, I, O, scratch):
    with ExitStack() as ctx:
        sem_names = []

        def sem(name):
            sem_names.append(name)
            return ctx.enter_context(nc.semaphore(name))

        at = {}

        def sb(name, shape, dt, offset):
            size = int(np.prod(shape[1:])) * 4
            assert offset + size <= 229368, name
            at[name] = (offset, offset + size)
            return nc.alloc_sbuf_tensor_at(name, shape, dt, offset=offset)

        B0 = 16512
        act_hi = sb("act_hi", [P, KT, T], F32R, B0)
        act_lo = sb("act_lo", [P, KT, T], F32R, B0 + 20480)
        raw = sb("raw", [P, 2, KT, 256], F32, B0 + 40960)
        w_hi = sb("w_hi", [P, 2, KT, P], F32R, B0 + 73728)
        w_lo = sb("w_lo", [P, 2, KT, P], F32R, B0 + 90112)
        C0 = B0 + 106496
        ident = sb("ident", [P, P], F32, C0)
        ones = sb("ones", [P, P], F32, C0 + 512)
        cols = sb("cols", [P, 96], F32, C0 + 1024)
        stat = sb("stat", [P, 16], F32, C0 + 1408)
        M0 = C0 + 1536
        sT = sb("sT", [P, 2 * NQ, NS], F32, M0)
        sV = sb("sV", [NS, NQ, HD], F32, M0 + 10240)
        o_hi = sb("o_hi", [P, HF + HG, T], F32R, M0 + 20480)
        o_lo = sb("o_lo", [P, HF + HG, T], F32R, M0 + 35840)
        X0 = M0 + 51200
        pT = sb("pT", [P, 24, SEQ], F32, X0)
        pV = sb("pV", [P, 2, 12, HD], F32, X0 + 24576)
        Y0 = X0 + 24576 + 12288
        x_nat = sb("x_nat", [P, 3, DM], F32, X0)
        xT0 = sb("xT0", [P, KT, T], F32, X0 + 24576)
        picks = sb("picks", [NB + 1, NPICK], F32, M0 + 20480)
        tables = sb("tables", [NB + 1, HDIL], F32, M0)
        rvec = sb("rvec", [HG, NG, 384], F32, M0 + 64)
        colraw = sb("colraw", [96, P], F32, M0 + 4672)
        sq = sb("sq", [P, 2, T], F32, M0 + 5184)
        rstd = sb("rstd", [P, T], F32, M0 + 7744)
        ntmp = sb("ntmp", [P, 2, 4, T], F32, M0 + 9024)
        k_stage = sb("k_stage", [P, 2, 3, 256], F32, Y0)
        v_stage = sb("v_stage", [P, 2, T], F32, Y0 + 6144)
        lf = sb("lf", [P, 3, 8], F32, Y0 + 8704)
        lfw = sb("lfw", [P, 8, 24], F32, Y0 + 8800)
        wf = sb("wf", [P, KT, 8], F32, Y0 + 9568)
        wf_hi = sb("wf_hi", [P, KT, 8], F32R, Y0 + 10080)
        wf_lo = sb("wf_lo", [P, KT, 8], F32R, Y0 + 10592)
        bfb = sb("bfb", [P, 8], F32, Y0 + 11104)
        upper = sb("upper", [P, P], F32, Y0 + 11136)
        causal = sb("causal", [P, P], F32, Y0 + 11648)
        upb = sb("upb", [NS, NS], F32, Y0 + 12160)
        cTd = sb("cTd", [8, HF, SEQ], F32, X0 + 16384)
        cTs = sb("cTs", [8, SEQ], F32, Y0 + 5120)
        negones = sb("negones", [8, P], F32, Y0 + 6144)
        pr = sb("pr", [P, NG, 384], F32, Y0)
        f_pt = sb("f_pt", [P, 384], F32, Y0 + 1536)
        f_q = sb("f_q", [P, SEQ], F32, Y0 + 3072)
        f_v = sb("f_v", [P, 2, HD], F32, Y0 + 4096)
        d_pt = sb("d_pt", [P, 384], F32, Y0 + 4608)
        d_v = sb("d_v", [P, 2, HD], F32, Y0 + 6144)
        d_q = sb("d_q", [P, NG, SEQ], F32, Y0 + 7168)
        d_h = sb("d_h", [P, NG, SEQ], F32, Y0 + 10240)
        rev = sb("rev", [P, P], F32, Y0 + 13312 + 32)
        sbias = sb("sbias", [P, 96], F32, Y0 + 13856 + 0)
        nbias = sb("nbias", [NS, 96], F32, Y0 + 14240)
        gkeep = sb("gkeep", [NS, 8], F32, Y0 + 14624)
        Z = X0
        kraw = sb("kraw", [P, 3, 1024], F32, Z)
        vraw = sb("vraw", [P, 3, 1024], F32, Z + 12288)
        kT = sb("kT", [P, 2, 1024], F32, Z + 24576)
        pf = sb("pf", [P, NPG, HF, DT], F32, Z + 32768)
        assert Z + 36864 == Y0
        bk = sb("bk", [P, HF, DB, NPG], F32, Y0)
        sn = sb("sn", [NS, NQ, NS], F32, Y0 + 4096)
        pd = sb("pd", [P, 96], F32, Y0 + 9216)
        m1 = sb("m1", [P, 96], F32, Y0 + 9600)
        mb = sb("mb", [P, 96], F32, Y0 + 9984)
        dg = sb("dg", [96, 96], F32, Y0 + 10368)
        rl = sb("rl", [P, 96], F32, Y0 + 10752)
        pn = sb("pn", [NS, NQ, DT], F32, Y0 + 11136)
        qb = sb("qb", [P, NQ, DT], F32, Y0 + 11776)
        nm = sb("nm", [NS, 32], F32, Y0 + 12416)
        ot = sb("ot", [P, 96], F32, Y0 + 12544)
        mx = sb("mx", [96, 1], F32, Y0 + 12928)
        blk = sb("blk", [NS, NS], F32, Y0 + 12960)
        tab = sb("tab", [1, P], I32, Y0 + 13344)
        g_stage = sb("g_stage", [P, T], F32, Y0 + 14656)
        lfp = sb("lfp", [P, 1024], F32, Z)
        lft = sb("lft", [P, HF, DB, NPG], F32, Z + 4096)
        lfs = sb("lfs", [P, HF, DB, NPG], F32, Z + 8192)
        low = sb("low", [P, P], F32, Z + 12288)
        tcol = sb("tcol", [P, 1], U32, Z + 12800)
        gates = sb("gates", [P, 2 * KT, T], F32, X0)
        mtmp = sb("mtmp", [P, 2, 2, T], F32, M0)
        outT = sb("outT", [P, KT, T], F32, X0)
        xT = sb("xT", [P, KT, T], F32, X0 + 20480)
        q_hi = sb("q_hi", [P, KQ, T], F32R, M0)
        q_lo = sb("q_lo", [P, KQ, T], F32R, M0 + 14080)
        a_hi = sb("a_hi", [P, KQ, T], F32R, B0)
        a_lo = sb("a_lo", [P, KQ, T], F32R, B0 + 20480)
        hid = sb("hid", [P, FB, T], F32, M0 + 34560)
        yacc = sb("yacc", [P, KT, T], F32, M0 + 28160)
        sig = sb("sig", [P, 2, T], F32, M0 + 90880)
        gs = sb("gs", [P, 2, T], F32, M0 + 90880 + 2560)
        x1T = sb("x1T", [P, KT, T], F32, M0 + 48640)
        y_nat = sb("y_nat", [P, 3, DM], F32, M0 + 69120)
        ps = ctx.enter_context(nc.psum_tensor("ps", [P, 8, 512], F32))

        in_x, in_cols, in_pick, in_lf = sem("in_x"), sem("in_cols"), sem("in_pick"), sem("in_lf")
        neg_row = sem("neg_row")
        cols_t, cols_ok = sem("cols_t"), sem("cols_ok")
        x_tr, x_evd, x_eva = sem("x_tr"), sem("x_evd"), sem("x_eva")
        bias_mm, bias_ev, rvec_st, hank_st = sem("bias_mm"), sem("bias_ev"), sem("rvec_st"), sem("hank_st")
        sq_ready, ss_mm, rms_d, rms_a = sem("sq_ready"), sem("ss_mm"), sem("rms_d"), sem("rms_a")
        nrm_ready, nrm_hi, nrm_done = sem("nrm_ready"), sem("nrm_hi"), sem("nrm_done")
        xT_spill = sem("xT_spill")
        wf_h, wf_l, f_mm, lf_z, lf_exp, lf_ok, out_lf = [sem(x) for x in (
            "wf_h", "wf_l", "f_mm", "lf_z", "lf_exp", "lf_ok", "out_lf")]
        raw_ld = [sem("raw_ld0"), sem("raw_ld1")]
        hi_done, lo_done = sem("hi_done"), sem("lo_done")
        unit_done = sem("unit_done")
        acc_free = sem("acc_free")
        nat_t, nat_ev = sem("nat_t"), sem("nat_ev")
        k_out = [sem("k_out0"), sem("k_out1")]
        v_out = sem("v_out")
        vchain = sem("vchain")
        pa_pre, pa_cum, pa_free, pa_q, pa_v = sem("pa_pre"), sem("pa_cum"), sem("pa_free"), sem("pa_q"), sem("pa_v")
        pa_s, pa_m, pa_e, pa_p, pa_t, pa_c, pa_o = [sem(f"pa_{x}") for x in "smeptco"]
        pd_c, pd_h, pd_free, pd_q, pd_v = sem("pd_c"), sem("pd_h"), sem("pd_free"), sem("pd_q"), sem("pd_v")
        pd_s, pd_m, pd_e, pd_p, pd_t, pd_pc, pd_o = [sem(f"pd_{x}") for x in ("s", "m", "e", "p", "t", "pc", "o")]
        tab_ld, lfp_ld, lft_t, lft_ok, lfs_ok, bk_mm, sn_mm, pre_ok = [sem(x) for x in (
            "tab_ld", "lfp_ld", "lft_t", "lft_ok", "lfs_ok", "bk_mm", "sn_mm", "pre_ok")]
        k_ld = [sem(f"k_ld{i}") for i in range(3)]
        v_ld = [sem(f"v_ld{i}") for i in range(3)]
        tr_a, tr_b, kt_a, kt_b = sem("tr_a"), sem("tr_b"), sem("kt_a"), sem("kt_b")
        sc_done, pv_done, qb_ok, s_read = sem("sc_done"), sem("pv_done"), sem("qb_ok"), sem("s_read")
        m1_ok, mt_ok, dg_ok, mb_mm, sub_ok, p_ok, l1_ok, sum_mm, rl_ok, o_done, o_ev = [sem(x) for x in (
            "m1_ok", "mt_ok", "dg_ok", "mb_mm", "sub_ok", "p_ok", "l1_ok", "sum_mm", "rl_ok", "o_done", "o_ev")]
        g_st, g_ld, g_sig = sem("g_st"), sem("g_ld"), sem("g_sig")
        xT_ld, x1_st, sg_done, q_h, q_l, x1_ld = [sem(x) for x in ("xT_ld", "x1_st", "sg_done", "q_h", "q_l", "x1_ld")]
        y_tr, y_evd, y_eva, y_out, win_out = sem("y_tr"), sem("y_evd"), sem("y_eva"), sem("y_out"), sem("win_out")

        w_in, w_gate, w_out = I["w_in"][0], I["w_gate"][0], I["w_out"][0]
        w_up, w_down = I["w_gate_up"][0], I["w_down"][0]

        def kblocks(w):
            return w.rearrange("(k p) n -> p k n", p=P)

        V_PAGES = range(KPG)
        SLOT_LOADS = [8, 8, 7]

        def ring_back(s):
            return 3 if s >= 3 else (2, 2, 5)[s]

        def kt_back(s):
            return 2 if s >= 2 else (1, 3)[s]

        def wait_pos(eng, s, value):
            if not isinstance(value, int) or value > 0:
                eng.wait_ge(s, value)

        def page_loaded(b, s):
            return b * (16 * SLOT_LOADS[s % 3]) + 16 * (s // 3 + 1)

        def n_b(b, s):
            return b * (KPG - 1) + (s if s <= NPG else s - 1)

        def dil_blocks(s):
            if s == NPG:
                return [(h, 0, h, 0, 1) for h in range(HG)]
            if s <= NPG + 2:
                return [(r * HG + h, 1, h, (s - NPG - 1) * 2 + r, 4) for r in range(2) for h in range(HG)]
            return [(r * HG + h, 2, h, (s - NPG - 3) * 2 + r, 8) for r in range(2) for h in range(HG)]

        block = ctx.enter_context(nc.Block())

        @block.sync
        def _(sp):
            sp.dma_start(ident[:], I["shape_consts"][:, C_ID:C_ID + P]).then_inc(in_cols, 16)
            for n, name in enumerate(("norm_pre_mix", "norm_post_mix", "norm_pre_ffn", "norm_post_ffn")):
                sp.dma_start(colraw[16 * n:16 * n + 16, :],
                             I[name][0].rearrange("(k p) -> k p", p=P)).then_inc(in_cols, 16)
            sp.dma_start(colraw[64:96, :], I["b_gate"][0].rearrange("(k p) -> k p", p=P)).then_inc(in_cols, 16)
            xp = I["x_prompt"][0].rearrange("(t p) d -> p t d", p=P)
            xs = I["x_sample"].rearrange("b t d -> (b t) d")
            sp.dma_start(x_nat[:, 0, :], xp[:, 0, :]).then_inc(in_x, 16)
            sp.dma_start(x_nat[:, 1, :], xp[:, 1, :]).then_inc(in_x, 16)
            sp.dma_start(x_nat[0:NS, 2, :], xs).then_inc(in_x, 16)

            def load_panel(slot, free, parts):
                wait_pos(sp, lo_done, free)
                for k0, src in parts:
                    sp.dma_start(raw[:, slot, k0:k0 + src.shape[1], :], src).then_inc(raw_ld[slot], 16)

            def cols_of(w, c, k0, k1):
                return kblocks(w)[:, k0:k1, bass.ds(c, 256)]

            def stream(u0, units, column):
                with sp.Fori(0, units // 4) as i:
                    for s in range(2):
                        w, c = column(i, s)
                        load_panel(s, i * 4 + (u0 + 2 * s - 2), [(0, cols_of(w, c, 0, 8)), (8, cols_of(w, c, 8, KT))])

            for s in range(2):
                load_panel(s, 0, [(0, cols_of(w_in, 256 * s, 0, 8)), (8, cols_of(w_in, 256 * s, 8, KT))])
            stream(4, U_DQ - 4, lambda i, s: (w_in, i * 512 + (512 + 256 * s)))
            stream(U_DQ, U_GATE - U_DQ, lambda i, s: (w_in, i * 512 + (3 * HF * HD + HF + 256 * s)))
            stream(U_GATE, 2 * KT, lambda i, s: (w_gate, i * 512 + 256 * s))
            wof, wod = kblocks(I["w_o_fox"][0]), kblocks(I["w_o_dil"][0])
            with sp.Fori(0, KT // 4) as i:
                for s in range(2):
                    c = i * 512 + 256 * s
                    load_panel(s, i * 4 + (U_O + 2 * s - 2), [(0, wof[:, :, bass.ds(c, 256)]), (8, wod[:, :, bass.ds(c, 256)])])
            stream(U_OUT, KT, lambda i, s: (w_out, i * 512 + 256 * s))
            stream(U_UP, 2 * FB, lambda i, s: (w_up, i * 256 + DFF * s))
            for kq in range(4):
                k0 = kq * KQ
                with sp.Fori(0, KT // 4) as i:
                    for s in range(2):
                        c = i * 512 + 256 * s
                        load_panel(s, i * 4 + (U_DOWN + 16 * kq + 2 * s - 2),
                                   [(0, cols_of(w_down, c, k0, k0 + 8)), (8, cols_of(w_down, c, k0 + 8, k0 + KQ))])
            yp = O["y_prompt"][0].rearrange("(t p) d -> p t d", p=P)
            ys = O["y_sample"].rearrange("b t d -> (b t) d")
            for t in range(3):
                sp.wait_ge(y_evd, 2 * t + 2)
                sp.wait_ge(y_eva, 2 * t + 2)
                if t < 2:
                    sp.dma_start(yp[:, t, :], y_nat[:, t, :]).then_inc(y_out, 16)
                else:
                    sp.dma_start(ys, y_nat[0:NS, 2, :]).then_inc(y_out, 16)
            sp.wait_ge(y_out, 48)

        @block.gpsimd
        def _(pool):
            consts = I["shape_consts"]
            pool.memset(ones[:], 1.0).then_inc(neg_row, 1)
            pool.wait_ge(neg_row, 1)
            pool.memset(tables[NB:NB + 1, :], NEG).then_inc(neg_row, 1)
            pool.dma_start(picks[:], I["bucket_picks"]).then_inc(in_pick, 16)
            pool.dma_start(tables[0:NB, :], I["rel_bias_table"]).then_inc(in_pick, 16)
            pool.dma_start(wf[:], kblocks(w_in)[:, :, 3 * HF * HD:3 * HF * HD + HF], ).then_inc(in_lf, 16)
            pool.dma_start(bfb[:], I["b_forget"].partition_broadcast(P).rearrange("p o h -> p (o h)")).then_inc(in_lf, 16)
            pool.dma_start(upper[:], consts[:, C_UP:C_UP + P]).then_inc(in_lf, 16)
            pool.dma_start(causal[:], consts[:, C_CAUSAL:C_CAUSAL + P]).then_inc(in_lf, 16)
            pool.dma_start(upb[:], consts[0:NS, C_UPB:C_UPB + NS]).then_inc(in_lf, 16)
            pool.wait_ge(x_evd, 6)
            pool.wait_ge(x_eva, 6)
            pool.dma_start(scratch["xT"].rearrange("k p t -> p k t"), xT0[:]).then_inc(xT_spill, 16)
            pool.wait_ge(bias_ev, 3)
            pool.dma_start(scratch["rvec"].rearrange("h g n -> h (g n)"), rvec[:].rearrange("h g n -> h (g n)")).then_inc(rvec_st, 16)
            pool.wait_ge(rvec_st, 16)
            r = scratch["rvec"]
            for h in range(HG):
                shifted = bass.AP(r.tensor, r.offset + h * NG * 384, [[1, P], [384, NG], [1, SEQ]])
                pool.dma_start(scratch["hankel"][h], shifted).then_inc(hank_st, 16)
            pool.wait_ge(lf_ok, 1)
            pool.dma_start(O["fox_logf_prompt"][0, 0].rearrange("(t p) h -> p t h", p=P), lf[:, 0:2, :]).then_inc(out_lf, 16)
            pool.dma_start(O["fox_logf_sample"][0].rearrange("b t h -> (b t) h"), lf[0:NS, 2, :]).then_inc(out_lf, 16)

            kp = O["fox_k_prompt"][0, 0].rearrange("(t p) h d -> p t (h d)", p=P)
            ks = O["fox_k_sample"][0].rearrange("b t h d -> (b t) (h d)")
            with pool.Fori(0, 2) as i:
                for s in range(2):
                    pool.wait_ge(nat_ev, i * 4 + (2 * s + 2))
                    c = i * 512 + 256 * s
                    pool.dma_start(kp[:, :, bass.ds(c, 256)], k_stage[:, s, 0:2, :]).then_inc(k_out[s], 16)
                    pool.dma_start(ks[:, bass.ds(c, 256)], k_stage[0:NS, s, 2, :]).then_inc(k_out[s], 16)
            pool.wait_ge(nat_ev, 16)
            pool.dma_start(O["fox_v_prompt"][0, 0].rearrange("(t p) h d -> p t (h d)", p=P),
                           pV[:, :, 0:HF, :].rearrange("p t h d -> p t (h d)")).then_inc(v_out, 16)
            pool.dma_start(O["fox_v_sample"][0].rearrange("b t h d -> (b t) (h d)"),
                           sV[:, 0:HF, :].rearrange("p h d -> p (h d)")).then_inc(v_out, 16)

            pool.wait_ge(k_out[0], 64)
            pool.wait_ge(k_out[1], 64)
            with pool.Fori(0, HF) as h:
                pool.wait_ge(pa_free, h + 1)
                pool.tensor_copy(f_q[:], pT[:, bass.ds(h, 1), :].rearrange("p o n -> p (o n)")).then_inc(pa_q, 1)
                pool.tensor_copy(f_v[:], pV[:, :, bass.ds(h, 1), :].rearrange("p t o d -> p t (o d)")).then_inc(pa_v, 1)

            for g in range(NG):
                for s in range(2):
                    pool.wait_ge(nat_ev, 16 + 4 * g + 2 * s + 2)
                    kd = O[f"win{g + 1}_k_prompt"][0, 0].rearrange("(t p) h d -> p t (h d)", p=P)[:, :, 256 * s:256 * s + 256]
                    rows = k_stage[:, s, 2 - kd.shape[1]:2, :]
                    pool.dma_start(kd, rows).then_inc(k_out[s], 16)
                    pool.dma_start(scratch["kd"][:, 512 * g + 256 * s:512 * g + 256 * s + 256],
                                   k_stage[0:NS, s, 2, :]).then_inc(k_out[s], 16)
            pool.wait_ge(nat_ev, 40)
            for g in range(NG):
                vd = O[f"win{g + 1}_v_prompt"][0, 0].rearrange("(t p) h d -> p t (h d)", p=P)
                pool.dma_start(vd, pV[:, 2 - vd.shape[1]:2, HG * g:HG * g + HG, :].rearrange("p t h d -> p t (h d)")).then_inc(v_out, 16)
            pool.dma_start(scratch["vd"], sV[:, HF:NQ, :].rearrange("p h d -> p (h d)")).then_inc(v_out, 16)

            pool.wait_ge(out_lf, 32)
            pool.wait_ge(k_out[0], 160)
            pool.wait_ge(k_out[1], 160)
            pool.dma_start(rev[:], consts[:, C_REV:C_REV + P]).then_inc(pd_c, 16)
            pool.wait_ge(hank_st, 64)
            qg = pT[:, 0:HDIL, :].rearrange("p (g h) n -> p g h n", g=NG)
            with pool.Fori(0, HG) as h:
                pool.wait_ge(pd_free, h + 1)
                pool.dma_start(d_h[:], scratch["hankel"][bass.ds(h, 1)].rearrange("o p g n -> (o p) g n")).then_inc(pd_h, 16)
                pool.tensor_copy(d_q[:], qg[:, :, bass.ds(h, 1), :].rearrange("p g o n -> p g (o n)")).then_inc(pd_q, 1)
                for g in range(NG):
                    if g:
                        pool.wait_ge(pd_o, h * NG + g)
                    pool.tensor_copy(d_v[:], pV[:, :, bass.ds(h + HG * g, 1), :].rearrange("p t o d -> p t (o d)")).then_inc(pd_v, 1)

            pool.wait_ge(pd_free, HG + 1)
            pool.wait_ge(v_out, 16 * 6)
            flat = I["page_table"].rearrange("b n -> (b n)")
            pool.dma_start(tcol[:], flat.rearrange("(n o) -> n o", o=1).bitcast(U32)).then_inc(tab_ld, 16)
            pool.dma_start(tab[:], flat.rearrange("(o n) -> o n", o=1)).then_inc(tab_ld, 16)
            pool.dma_start(low[:], consts[:, C_LOW:C_LOW + P]).then_inc(tab_ld, 16)
            pool.dma_start(blk[:], consts[0:NS, C_BLK:C_BLK + NS]).then_inc(tab_ld, 16)
            pool.wait_ge(tab_ld, 64)
            pool.indirect_dma_start(lfp[:], None, I["cache_fox_logf"][0].rearrange("n t h -> n (t h)"),
                                    bass.IndirectOffsetOnAxis(ap=tcol[:, 0:1], axis=0)).then_inc(lfp_ld, 16)
            pool.wait_ge(pre_ok, 1)

            pages = [I[f"cache_fox_{x}"][0].rearrange("n t h d -> n t (h d)") for x in "kv"]
            wins = [[I[f"cache_win{g + 1}_{x}"][0].rearrange("b (p r) h d -> b p (r h d)", p=P) for g in range(NG)] for x in "kv"]

            def load_page(kv, b, s):
                dst = (kraw, vraw)[kv][:, s % 3, :]
                done = (k_ld, v_ld)[kv][s % 3]
                n = b * KPG + s
                back = n - ring_back(s)
                if kv:
                    pool.wait_ge(pv_done, back + 4)
                else:
                    wait_pos(pool, tr_a, back + 1)
                    back_b = n_b(b, s - 3) + (s - 3 != NPG) if s >= 3 else n_b(b, 0) - (1, 0, 2)[s]
                    wait_pos(pool, tr_b, back_b)
                if s < NPG:
                    page = pool.value_load(tab[0:1, bass.ds(b * NPG + s, 1)], min_val=0, max_val=I["cache_fox_k"].shape[1] - 1)
                    pool.dma_start(dst, pages[kv][bass.ds(page, 1)].rearrange("o t c -> t (o c)")).then_inc(done, 16)
                    return
                g, c, width = (0, 0, 512) if s == NPG else (1, (s - NPG - 1) * 1024, 1024) if s <= NPG + 2 else (2, (s - NPG - 3) * 1024, 1024)
                pool.dma_start(dst[:, 0:width], wins[kv][g][bass.ds(b, 1), :, c:c + width].rearrange("o p c -> p (o c)")).then_inc(done, 16)

            for s in range(KPG):
                load_page(0, 0, s)
            with pool.Fori(1, DB) as b:
                for s in range(KPG):
                    load_page(0, b, s)
                    load_page(1, b - 1, s)
            for s in range(KPG):
                load_page(1, DB - 1, s)

            pool.wait_ge(o_ev, DB)
            pool.wait_ge(g_st, 16 * 2 * KT)
            for n in range(4):
                pool.dma_start(gates[:, 8 * n:8 * n + 8, :], scratch["gates"][8 * n:8 * n + 8].rearrange("k p t -> p k t")).then_inc(g_ld, 16)
            pool.wait_ge(acc_free, U_OUT + 2)
            pool.dma_start(xT[:], scratch["xT"].rearrange("k p t -> p k t")).then_inc(xT_ld, 16)
            pool.wait_ge(nrm_done, 8)
            pool.dma_start(scratch["x1T"].rearrange("k p t -> p k t"), xT[:]).then_inc(x1_st, 16)

            n_win = 0
            for b in range(DB):
                pool.wait_ge(unit_done, U_UP + 18 * b + 1)
                for g, (window, _) in enumerate(DIL):
                    for x in "kv":
                        src = I[f"cache_win{g + 1}_{x}"][0, b].rearrange("w h d -> (w h d)")[DT * HG * HD:]
                        dst = O[f"win{g + 1}_{x}_sample"][0, b].rearrange("w h d -> (w h d)")[:(window - DT) * HG * HD]
                        pool.dma_start(dst.rearrange("(p n) -> p n", p=P), src.rearrange("(p n) -> p n", p=P)).then_inc(win_out, 16)
                        n_win += 1
                if b == 6:
                    pool.wait_ge(q_l, 3)
                    pool.wait_ge(x1_st, 16)
                    pool.dma_start(x1T[:], scratch["x1T"].rearrange("k p t -> p k t")).then_inc(x1_ld, 16)
            for g, (window, _) in enumerate(DIL):
                for x in "kv":
                    dst = O[f"win{g + 1}_{x}_sample"][0].rearrange("b w h d -> b w (h d)")[:, window - DT:window, :]
                    src = scratch[x + "d"].rearrange("(b t) c -> b t c", t=DT)[:, :, 512 * g:512 * g + 512]
                    pool.dma_start(dst, src).then_inc(win_out, 16)
                    n_win += 1
            pool.wait_ge(win_out, 16 * n_win)

        @block.tensor
        def _(pe):
            def unit(u, bank, x_hi, x_lo, blocks, slot, extra=None):
                pe.wait_ge(lo_done, u + 1)
                pe.wait_ge(acc_free, u + 1)
                for (k0, k1, bk_, xh, xl) in [(0, blocks, bank, x_hi, x_lo)] + (extra or []):
                    for k in range(k0, k1):
                        x_k = k - k0
                        pe.matmul(ps[:, bk_, 0:T], w_hi[:, slot, k, :], xh[:, x_k, :], start=(k == k0), stop=False)
                        pe.matmul(ps[:, bk_, 0:T], w_hi[:, slot, k, :], xl[:, x_k, :], start=False, stop=False)
                        mm = pe.matmul(ps[:, bk_, 0:T], w_lo[:, slot, k, :], xh[:, x_k, :], start=False, stop=(k == k1 - 1))
                mm.then_inc(unit_done, 1)

            def sum_squares(n):
                for k in range(KT):
                    pe.wait_ge(sq_ready, KT * n + k + 1)
                    pe.matmul(ps[:, 7, 0:T], ones[:], sq[:, k % 2, :], start=(k == 0), stop=(k == KT - 1)).then_inc(ss_mm, 1)

            pe.wait_ge(in_cols, 96)
            pe.transpose(ps[:, 7, 0:96], colraw[:], ident[0:96, 0:96]).then_inc(cols_t, 1)
            pe.wait_ge(in_x, 48)
            for n in range(12):
                t, q = divmod(n, 4)
                rows = P if t < 2 else NS
                if n >= 4:
                    pe.wait_ge(x_eva if n % 2 else x_evd, n // 2 - 1)
                for k in range(4):
                    mm = pe.transpose(ps[:, n % 4, rows * k:rows * k + rows],
                                      x_nat[0:rows, t, (4 * q + k) * P:(4 * q + k + 1) * P], ident[0:rows, 0:rows])
                mm.then_inc(x_tr, 1)
            pe.wait_ge(in_pick, 32)
            pe.wait_ge(neg_row, 2)
            rp = picks[:, SPICK:].rearrange("p (g n) -> p g n", g=NG)
            for g in range(NG):
                mm = pe.matmul(ps[0:HG, 4 + g, 0:384], tables[:, HG * g:HG * g + HG], rp[:, g, :], start=True, stop=True)
                mm.then_inc(bias_mm, 1)
            pe.wait_ge(bias_ev, 2)
            sp_ = picks[:, 0:SPICK].rearrange("p (g q n) -> p g q n", g=NG, q=DT)
            for g in range(NG):
                for q in range(DT):
                    mm = pe.matmul(ps[:, 4, 32 * g + q:32 * g + 32:8], sp_[:, g, q, 0:P], tables[:, HG * g:HG * g + HG], start=True, stop=True)
                    if g == 0 and q < 2:
                        mm.then_inc(nat_t, 1)
                    mm = pe.matmul(ps[0:NS, 5, 32 * g + q:32 * g + 32:8], sp_[:, g, q, P:P + NS], tables[:, HG * g:HG * g + HG], start=True, stop=True)
            mm.then_inc(bias_mm, 1)
            pe.wait_ge(cols_ok, 1)
            sum_squares(0)

            pe.wait_ge(nrm_done, 4)
            pe.wait_ge(wf_l, 1)
            for t in range(3):
                rows = P if t < 2 else NS
                tok = slice(t * P, t * P + rows)
                for k in range(KT):
                    o = ps[0:rows, 6, 8 * t:8 * t + 8]
                    pe.matmul(o, act_hi[:, k, tok], wf_hi[:, k, :], start=(k == 0), stop=False)
                    pe.matmul(o, act_hi[:, k, tok], wf_lo[:, k, :], start=False, stop=False)
                    mm = pe.matmul(o, act_lo[:, k, tok], wf_hi[:, k, :], start=False, stop=(k == KT - 1))
            mm.then_inc(f_mm, 1)

            def turn(kvn, u, c):
                pe.wait_ge(acc_free, u + 3)
                if not isinstance(kvn, int) or kvn >= 2:
                    pe.wait_ge(nat_ev, kvn - 1)
                for t in range(3):
                    rows = P if t < 2 else NS
                    mm = pe.transpose(ps[0:rows, 4 + c, P * t:P * t + P], v_stage[:, c, t * P:t * P + rows], ident[:])
                mm.then_inc(nat_t, 1)

            def qkv(u0, kv0, q_trips, kv_trips):
                with pe.Fori(0, q_trips) as i:
                    for k in range(4):
                        unit(i * 4 + (u0 + k), k, act_hi, act_lo, KT, k % 2)
                u1 = u0 + 4 * q_trips
                for k in range(4):
                    unit(u1 + k, k, act_hi, act_lo, KT, k % 2)
                    if k >= 2:
                        turn(kv0 + k - 2, u1 + k - 2, k % 2)
                with pe.Fori(1, kv_trips) as i:
                    for k in range(4):
                        unit(i * 4 + (u1 + k), k, act_hi, act_lo, KT, k % 2)
                        turn(i * 4 + (kv0 + k - 2), i * 4 + (u1 + k - 2), k % 2)
                for k in range(2):
                    turn(kv0 + 4 * kv_trips + k - 2, u1 + 4 * kv_trips + k - 2, k % 2)

            qkv(U_FQ, 0, 2, 4)

            pe.wait_ge(lf_ok, 1)
            pe.wait_ge(in_lf, 80)
            pe.matmul(ps[0:8, 6, 0:P], lf[:, 0, :], upper[:], start=True, stop=True)
            pe.matmul(ps[0:8, 6, P:SEQ], lf[:, 0, :], ones[:], start=True, stop=False)
            pe.matmul(ps[0:8, 6, P:SEQ], lf[:, 1, :], upper[:], start=False, stop=True).then_inc(pa_cum, 1)
            pe.matmul(ps[0:NS, 7, 0:8], upb[:], lf[0:NS, 2, :], start=True, stop=True).then_inc(pa_cum, 1)
            pe.wait_ge(pa_pre, 1)
            mmx = dict(skip_group_check=True)
            with pe.Fori(0, HF) as h:
                keys = pT[:, bass.ds(h + HF, 1), :].rearrange("p o n -> p (o n)")
                cum = cTd[:, bass.ds(h, 1), :].rearrange("p o n -> p (o n)")
                pe.wait_ge(pa_q, h + 1)
                pe.matmul(ps[:, 0, 0:P], f_q[:, 0:P], keys[:, 0:P], start=True, stop=False, **mmx)
                pe.matmul(ps[:, 0, 0:P], negones[:], cum[:, 0:P], start=False, stop=False, **mmx)
                pe.matmul(ps[:, 0, 0:P], ident[:], causal[:], start=False, stop=False, **mmx)
                pe.matmul(ps[:, 0, P:384], f_q[:, P:SEQ], keys, start=False, stop=False, **mmx)
                pe.matmul(ps[:, 0, P:384], negones[:], cum, start=False, stop=False, **mmx)
                pe.matmul(ps[:, 0, SEQ:384], ident[:], causal[:], start=False, stop=True, **mmx).then_inc(pa_s, 1)
                pe.wait_ge(pa_p, h * 2 + 2)
                for j in range(3):
                    mm = pe.transpose(ps[:, 2, P * j:P * j + P], pr[:, 0, P * j:P * j + P], ident[:])
                mm.then_inc(pa_t, 1)
                pe.wait_ge(pa_c, h + 1)
                pe.wait_ge(pa_v, h + 1)
                pe.matmul(ps[:, 3, 0:SEQ], f_v[:, 0, :], f_pt[:, 0:SEQ], start=True, stop=False, **mmx)
                pe.matmul(ps[:, 3, P:SEQ], f_v[:, 1, :], f_pt[:, SEQ:384], start=False, stop=True, **mmx).then_inc(pa_o, 1)

            qkv(U_DQ, 16, 3, 6)

            pe.wait_ge(pd_c, 16)
            with pe.Fori(0, HG) as h:
                pe.wait_ge(pd_q, h + 1)
                pe.wait_ge(pd_h, h * 16 + 16)
                for g in range(NG):
                    keys = pT[:, bass.ds(h + (HDIL + HG * g), 1), :].rearrange("p o n -> p (o n)")
                    pe.matmul(ps[:, g, 0:P], d_q[:, g, 0:P], keys[:, 0:P], start=True, stop=False, **mmx)
                    pe.matmul(ps[:, g, 0:P], rev[:], d_h[:, g, P:SEQ], start=False, stop=False, **mmx)
                    pe.matmul(ps[:, g, P:384], d_q[:, g, P:SEQ], keys, start=False, stop=False, **mmx)
                    mm = pe.matmul(ps[:, g, P:384], rev[:], d_h[:, g, :], start=False, stop=True, **mmx)
                mm.then_inc(pd_s, 1)
                pe.wait_ge(pd_p, h * 2 + 2)
                for g in range(NG):
                    for j in range(3):
                        mm = pe.transpose(ps[:, 3 + g, P * j:P * j + P], pr[:, g, P * j:P * j + P], ident[:])
                    mm.then_inc(pd_t, 1)
                for g in range(NG):
                    pe.wait_ge(pd_pc, h * NG + (g + 1))
                    pe.wait_ge(pd_v, h * NG + (g + 1))
                    pe.matmul(ps[:, 6, 0:SEQ], d_v[:, 0, :], d_pt[:, 0:SEQ], start=(g == 0), stop=False, **mmx)
                    pe.matmul(ps[:, 6, P:SEQ], d_v[:, 1, :], d_pt[:, SEQ:384], start=False, stop=(g == NG - 1), **mmx).then_inc(pd_o, 1)

            pe.wait_ge(lfp_ld, 16)
            by_head = lfp[:].rearrange("p (t h) -> p h t", h=HF)
            for h in range(HF):
                mm = pe.transpose(ps[:, h // 4, P * (h % 4):P * (h % 4) + P], by_head[:, h, :], ident[:])
            mm.then_inc(lft_t, 1)
            for h in range(NQ):
                mm = pe.matmul(ps[0:NS, 4 + h // 8, NS * (h % 8):NS * (h % 8) + NS], sT[:, NQ + h, :], sT[:, h, :], start=True, stop=True)
                if h < 3:
                    mm.then_inc(pv_done, 1)
            mm.then_inc(sn_mm, 1)
            pe.wait_ge(lfs_ok, 1)
            for n in range(2):
                half = slice(4 * n, 4 * n + 4)
                pe.matmul(ps[:, 2 + n, :], low[:], lft[:, half].rearrange("p h b g -> p (h b g)"), start=True, stop=False)
                mm = pe.matmul(ps[:, 2 + n, :], ones[:], lfs[:, half].rearrange("p h b g -> p (h b g)"), start=False, stop=True)
            mm.then_inc(bk_mm, 1)
            pe.wait_ge(pre_ok, 1)

            def transposes(b, s):
                pe.wait_ge(k_ld[s % 3], page_loaded(b, s))
                wait_pos(pe, kt_a, b * KPG + s)
                for j in range(4):
                    mm = pe.transpose(ps[:, 2, P * j:P * j + P], kraw[:, s % 3, P * j:P * j + P], ident[:])
                mm.then_inc(tr_a, 1)
                if s != NPG:
                    wait_pos(pe, kt_b, n_b(b, s))
                    for j in range(4):
                        mm = pe.transpose(ps[:, 3, P * j:P * j + P], kraw[:, s % 3, P * (4 + j):P * (5 + j)], ident[:])
                    mm.then_inc(tr_b, 1)

            def scores(b, s):
                pe.wait_ge(kt_a, b * KPG + (s + 1))
                if s != NPG:
                    pe.wait_ge(kt_b, n_b(b, s) + 1)
                if s == 0:
                    pe.wait_ge(qb_ok, b + 1)
                    wait_pos(pe, s_read, b)
                if s == NPG:
                    wait_pos(pe, rl_ok, b)
                if s < NPG:
                    for h in range(HF):
                        mm = pe.matmul(ps[:, 4 + s // 8, 64 * (s % 8) + 8 * h:64 * (s % 8) + 8 * h + 8],
                                       kT[:, s % 2, P * h:P * h + P], qb[:, h, :], start=True, stop=True)
                else:
                    for r, g, h, q, step in dil_blocks(s):
                        mm = pe.matmul(ps[:, 6, 32 * g + 8 * h + q:32 * g + 8 * h + 8:step],
                                       kT[:, s % 2, P * r:P * r + P], qb[:, HF + HG * g + h, q:8:step], start=True, stop=True)
                mm.then_inc(sc_done, 1)

            def values(b, s):
                pe.wait_ge(v_ld[s % 3], page_loaded(b, s))
                if s == 0:
                    pe.wait_ge(p_ok, b * 3 + 3)
                    wait_pos(pe, o_ev, b)
                if s < NPG:
                    for h in range(HF):
                        mm = pe.matmul(ps[:, 7, 8 * h:8 * h + 8], vraw[:, s % 3, P * h:P * h + P], pf[:, s, h, :],
                                       start=(s == 0 and h == 0), stop=False, **mmx)
                else:
                    for r, g, h, q, step in dil_blocks(s):
                        mm = pe.matmul(ps[:, 7, 64 + 8 * h + q:64 + 8 * h + 8:step], vraw[:, s % 3, P * r:P * r + P],
                                       pd[:, 32 * g + 8 * h + q:32 * g + 8 * h + 8:step], start=False, stop=False, **mmx)
                mm.then_inc(pv_done, 1)

            def new_values(b):
                for h in range(NQ):
                    c = 8 * h if h < HF else 64 + 8 * ((h - HF) % HG)
                    mm = pe.matmul(ps[:, 7, c:c + 8], sV[:, h, :], pn[:, h, :], start=False, stop=(h == NQ - 1), **mmx)
                mm.then_inc(o_done, 1)

            def sequence(b):
                first = isinstance(b, int)
                for s in range(KPG):
                    transposes(b, s)
                    if s:
                        scores(b, s - 1)
                    if not first:
                        values(b - 1, s)
                scores(b, KPG - 1)
                if not first:
                    new_values(b - 1)
                u = b * 4 + U_GATE
                unit(u, 0, act_hi, act_lo, KT, 0)
                pe.wait_ge(m1_ok, b + 1)
                pe.transpose(ps[0:96, 6, 0:P], m1[:], ident[:]).then_inc(mt_ok, 1)
                unit(u + 1, 1, act_hi, act_lo, KT, 1)
                pe.wait_ge(dg_ok, b + 1)
                pe.matmul(ps[:, 6, P:P + 96], ones[0:96, :], dg[:], start=True, stop=True).then_inc(mb_mm, 1)
                unit(u + 2, 0, act_hi, act_lo, KT, 0)
                pe.wait_ge(l1_ok, b + 1)
                pe.matmul(ps[:, 6, 256:352], ones[:], m1[:], start=True, stop=True).then_inc(sum_mm, 1)
                unit(u + 3, 1, act_hi, act_lo, KT, 1)

            sequence(0)
            with pe.Fori(1, DB) as b:
                sequence(b)
            for s in range(KPG):
                values(DB - 1, s)
            new_values(DB - 1)

            pe.wait_ge(o_ev, DB)
            pe.wait_ge(rl_ok, DB)
            with pe.Fori(0, KT // 4) as i:
                for k in range(4):
                    unit(i * 4 + (U_O + k), k, o_hi, o_lo, HF, k % 2,
                         [(HF, HF + HG, 4 + k, o_hi[:, HF:, :], o_lo[:, HF:, :])])
            pe.wait_ge(acc_free, U_OUT + 2)
            with pe.Fori(0, KT // 4) as i:
                for k in range(4):
                    unit(i * 4 + (U_OUT + k), k, act_hi, act_lo, KT, k % 2)
            sum_squares(1)
            sum_squares(2)
            pe.wait_ge(nrm_done, 12)
            with pe.Fori(0, FB // 2) as i:
                for k in range(4):
                    unit(i * 4 + (U_UP + k), k, act_hi, act_lo, KT, k % 2)
            for kq in range(4):
                pe.wait_ge(q_l, kq + 1)
                xh, xl = (q_hi, q_lo) if kq % 2 == 0 else (a_hi, a_lo)
                with pe.Fori(0, KT // 4) as i:
                    for k in range(4):
                        unit(i * 4 + (U_DOWN + 16 * kq + k), k, xh, xl, KQ, k % 2)
            sum_squares(3)
            pe.wait_ge(nrm_done, 16)
            for n in range(12):
                t, q = divmod(n, 4)
                rows = P if t < 2 else NS
                if n >= 4:
                    pe.wait_ge(y_eva if n % 2 else y_evd, n // 2 - 1)
                for k in range(4):
                    mm = pe.transpose(ps[0:rows, n % 4, P * k:P * k + P], x1T[:, 4 * q + k, t * P:t * P + rows], ident[:])
                mm.then_inc(y_tr, 1)

        @block.scalar
        def _(act):
            def split_hi(slot, pslot, landed, kt=KT):
                act.wait_ge(raw_ld[pslot], landed)
                act.activation(w_hi[:, slot, 0:kt, :], raw[:, pslot, 0:kt, P * slot:P * slot + P], ACT.Copy).then_inc(hi_done, 1)

            def step(u, k, trip_loads, kt=KT):
                act.wait_ge(unit_done, u + 1)
                if k < 2:
                    split_hi(k % 2, 1, trip_loads + 32, kt)
                else:
                    split_hi(k % 2, 0, trip_loads + 64, kt)

            def loads(u):
                return u * 8

            def squares(n, src):
                for k in range(KT):
                    m = KT * n + k
                    if m >= 2:
                        act.wait_ge(ss_mm, m - 1)
                    act.activation(sq[:, k % 2, :], src[:, k, :], ACT.Square).then_inc(sq_ready, 1)

            def root(n):
                act.wait_ge(rms_d, 2 * n + 1)
                act.activation(rstd[:], rstd[:], ACT.Sqrt).then_inc(rms_a, 1)

            def high_parts(n0, dst):
                for q in range(4):
                    act.wait_ge(nrm_ready, n0 + q + 1)
                    act.activation(dst[:, 4 * q:4 * q + 4, :], ntmp[:, q % 2], ACT.Copy).then_inc(nrm_hi, 1)

            for n in range(1, 12, 2):
                t, q = divmod(n, 4)
                rows = P if t < 2 else NS
                act.wait_ge(x_tr, n + 1)
                act.activation(xT0[:, 4 * q:4 * q + 4, t * P:t * P + rows],
                               ps[:, n % 4, 0:4 * rows].rearrange("p (k r) -> p k r", k=4), ACT.Copy).then_inc(x_eva, 1)
            act.wait_ge(x_evd, 6)
            act.wait_ge(x_eva, 6)
            squares(0, xT0)
            root(0)
            for k in range(2):
                split_hi(k, 0, 32)
            high_parts(0, act_hi)
            act.wait_ge(in_lf, 80)
            act.activation(wf_hi[:], wf[:], ACT.Copy).then_inc(wf_h, 1)

            def nat_rows(kvn, c, pslot, to_k, h):
                act.wait_ge(nat_t, kvn + 3)
                tiles = ps[:, 4 + c, 0:SEQ].rearrange("p (t d) -> p t d", t=2)
                if to_k:
                    act.activation(k_stage[:, pslot, 0:2, P * c:P * c + P], tiles, ACT.Copy)
                    act.activation(k_stage[0:NS, pslot, 2, P * c:P * c + P], ps[0:NS, 4 + c, SEQ:384], ACT.Copy).then_inc(nat_ev, 1)
                else:
                    hp, hs = h
                    act.activation(pV[:, :, bass.ds(hp, 1), :].rearrange("p t o d -> p t (o d)"), tiles, ACT.Copy)
                    act.activation(sV[:, bass.ds(hs, 1), :].rearrange("p o d -> p (o d)"), ps[0:NS, 4 + c, SEQ:384], ACT.Copy).then_inc(nat_ev, 1)

            def qkv(u0, kv0, n, sv0, stored):
                with act.Fori(0, n // 4) as i:
                    for k in range(4):
                        step(i * 4 + (u0 + k), k, i * 32 + loads(u0))
                uk = u0 + n

                def trip(i, first_kind, second_kind):
                    for k in range(4):
                        step(i * 4 + (uk + k), k, i * 32 + loads(uk))
                        kind = first_kind if k < 2 else second_kind
                        if kind is None:
                            continue
                        j = i * 4 + (k - 2)
                        slot = 1 if k < 2 else 0
                        if kind == "k" and k % 2 == 0:
                            v = (i * 32 + (stored - 32)) if slot == 1 else (i * 32 + stored)
                            if not (isinstance(v, int) and v <= 0):
                                act.wait_ge(k_out[slot], v)
                        nat_rows(j + kv0, k % 2, slot, kind == "k", (j - n, j - n + sv0))

                kt, vt = n // 4, n // 4
                trip(0, None, "k")
                with act.Fori(1, kt) as i:
                    trip(i, "k", "k")
                trip(kt, "k", "v")
                with act.Fori(kt + 1, kt + vt) as i:
                    trip(i, "v", "v")
                for k in range(2):
                    j = 4 * (kt + vt) + k - 2
                    nat_rows(j + kv0, k % 2, 1, False, (j - n, j - n + sv0))

            act.wait_ge(lf_z, 1)
            act.activation(lfw[:, 2, :], lfw[:, 1, :], ACT.Exp, scale=-1.0).then_inc(lf_exp, 1)
            act.wait_ge(xT_spill, 16)
            qkv(U_FQ, 0, HF, 0, 0)

            with act.Fori(0, HF) as h:
                act.wait_ge(pa_m, h * 2 + 2)
                act.activation(pr[:, 0, 0:P], ps[:, 0, 0:P], ACT.Exp, bias=stat[:, 0:1], accum_out=stat[:, 2:3]).then_inc(pa_e, 1)
                act.activation(pr[:, 0, P:384], ps[:, 0, P:384], ACT.Exp, bias=stat[:, 1:2], accum_out=stat[:, 3:4]).then_inc(pa_e, 1)
                act.wait_ge(pa_t, h + 1)
                act.activation(f_pt[:], ps[:, 2, 0:384], ACT.Copy).then_inc(pa_c, 1)
            act.wait_ge(v_out, 32)
            qkv(U_DQ, 16, HDIL, HF, 64)

            with act.Fori(0, HG) as h:
                act.wait_ge(pd_m, h * 2 + 2)
                act.activation(pr[:, :, 0:P], ps[:, 0:NG, 0:P], ACT.Exp, bias=stat[:, 0:1], accum_out=stat[:, 2:3]).then_inc(pd_e, 1)
                act.activation(pr[:, :, P:384], ps[:, 0:NG, P:384], ACT.Exp, bias=stat[:, 1:2], accum_out=stat[:, 3:4]).then_inc(pd_e, 1)
                for g in range(NG):
                    act.wait_ge(pd_t, h * NG + (g + 1))
                    if g:
                        act.wait_ge(pd_o, h * NG + g)
                    act.activation(d_pt[:], ps[:, 3 + g, 0:384], ACT.Copy).then_inc(pd_pc, 1)

            def keys_a(b, s):
                act.wait_ge(tr_a, b * KPG + (s + 1))
                wait_pos(act, sc_done, b * KPG + (s - kt_back(s) + 1))
                act.activation(kT[:, s % 2, 0:512], ps[:, 2, :], ACT.Copy).then_inc(kt_a, 1)

            def store_gate(g):
                act.wait_ge(acc_free, g + (U_GATE + 3))
                act.dma_start(scratch["gates"][bass.ds(g, 1)].rearrange("o p t -> (o p) t"), g_stage[:]).then_inc(g_st, 16)

            act.wait_ge(pre_ok, 1)

            def sequence(b):
                for s in range(KPG):
                    keys_a(b, s)
                g, ld = b * 4, b * 32 + loads(U_GATE)
                step(g + U_GATE, 0, ld)
                store_gate(g)
                step(g + (U_GATE + 1), 1, ld)
                store_gate(g + 1)
                act.wait_ge(sub_ok, b + 1)
                act.activation(pf[:], pf[:], ACT.Exp).then_inc(p_ok, 1)
                act.activation(pd[:], pd[:], ACT.Exp).then_inc(p_ok, 1)
                act.activation(pn[:], pn[:], ACT.Exp).then_inc(p_ok, 1)
                step(g + (U_GATE + 2), 2, ld)
                store_gate(g + 2)
                step(g + (U_GATE + 3), 3, ld)
                store_gate(g + 3)

            sequence(0)
            with act.Fori(1, DB) as b:
                sequence(b)

            for n in range(4):
                act.wait_ge(g_ld, 64)
                act.activation(gates[:, 8 * n:8 * n + 8, :], gates[:, 8 * n:8 * n + 8, :], ACT.Sigmoid).then_inc(g_sig, 1)
            for u0, n in ((U_O, 4), (U_OUT, 4)):
                with act.Fori(0, n) as i:
                    for k in range(4):
                        step(i * 4 + (u0 + k), k, i * 32 + loads(u0))
            act.wait_ge(acc_free, U_UP + 2)
            squares(1, outT)
            root(1)
            act.wait_ge(nrm_done, 8)
            squares(2, xT)
            root(2)
            high_parts(4, act_hi)

            act.wait_ge(x1_st, 16)
            with act.Fori(0, FB // 2) as i:
                for k in range(4):
                    step(i * 4 + (U_UP + k), k, i * 32 + loads(U_UP))
                    if k < 2:
                        act.activation(sig[:, k, :], ps[:, k, 0:T], ACT.Sigmoid).then_inc(sg_done, 1)

            def quarter_hi(kq):
                dst = a_hi if kq % 2 else q_hi
                act.activation(dst[:], hid[:, KQ * kq:KQ * kq + KQ, :], ACT.Copy).then_inc(q_h, 1)

            act.wait_ge(acc_free, U_DOWN + 2)
            quarter_hi(0)
            for kq in range(4):
                u0 = U_DOWN + 16 * kq
                with act.Fori(0, 2) as i:
                    for k in range(4):
                        step(i * 4 + (u0 + k), k, i * 32 + loads(u0), KQ)
                if kq < 3:
                    quarter_hi(kq + 1)
                    with act.Fori(2, 4) as i:
                        for k in range(4):
                            step(i * 4 + (u0 + k), k, i * 32 + loads(u0), KQ)
                else:
                    for k in range(4):
                        step(u0 + 8 + k, k, loads(u0 + 8), KQ)
                    for k in range(2):
                        step(u0 + 12 + k, k, loads(u0 + 12), KQ)
            act.wait_ge(acc_free, U_END + 2)
            squares(3, yacc)
            root(3)
            for n in range(1, 12, 2):
                t, q = divmod(n, 4)
                rows = P if t < 2 else NS
                act.wait_ge(y_tr, n + 1)
                act.activation(y_nat[0:rows, t, 512 * q:512 * q + 512], ps[0:rows, n % 4, :], ACT.Copy).then_inc(y_eva, 1)

        @block.vector
        def _(dve):
            ch = Tally(vchain)

            def link(ins):
                ch.inc(ins)
                ch.wait(dve)

            def split_lo(slot, pslot, u, kt=KT):
                dve.wait_ge(hi_done, u + 1)
                half = slot
                dve.tensor_tensor(w_lo[:, slot, 0:kt, :], raw[:, pslot, 0:kt, P * half:P * half + P],
                                  w_hi[:, slot, 0:kt, :].bitcast(F32), ALU.subtract).then_inc(lo_done, 1)

            def step(u, k, kt=KT):
                dve.wait_ge(unit_done, u + 1)
                split_lo(k % 2, 1 if k < 2 else 0, u + 2, kt)

            def rms(n):
                dve.wait_ge(ss_mm, KT * n + KT)
                dve.tensor_scalar(rstd[:], ps[:, 7, 0:T], 1.0 / DM, EPS, ALU.mult, ALU.add).then_inc(rms_d, 1)
                dve.wait_ge(rms_a, n + 1)
                dve.reciprocal(rstd[:], rstd[:]).then_inc(rms_d, 1)
                dve.wait_ge(rms_d, 2 * n + 2)

            def normed(dst, src, c, k):
                return dve.scalar_tensor_tensor(out=dst, in0=src, scalar=cols[:, c + k:c + k + 1], in1=rstd[:],
                                                op0=ALU.mult, op1=ALU.mult)

            def norm_split(n0, src, c, m0):
                for q in range(4):
                    if q >= 2:
                        ch.wait(dve)
                    for k in range(4):
                        ins = normed(ntmp[:, q % 2, k, :], src[:, 4 * q + k, :], c, 4 * q + k)
                        ch.inc(ins) if k < 3 else ins.then_inc(nrm_ready, 1)
                    dve.wait_ge(nrm_hi, n0 + q + 1)
                    dve.wait_ge(nrm_ready, n0 + q + 1)
                    dve.tensor_tensor(act_lo[:, 4 * q:4 * q + 4, :], ntmp[:, q % 2], act_hi[:, 4 * q:4 * q + 4, :].bitcast(F32),
                                      ALU.subtract).then_inc(nrm_done, 1)
                dve.wait_ge(nrm_done, m0 + 4)

            dve.wait_ge(cols_t, 1)
            dve.tensor_copy(cols[:], ps[:, 7, 0:96]).then_inc(cols_ok, 1)
            for n in range(0, 12, 2):
                t, q = divmod(n, 4)
                rows = P if t < 2 else NS
                dve.wait_ge(x_tr, n + 1)
                dve.tensor_copy(xT0[:, 4 * q:4 * q + 4, t * P:t * P + rows],
                                ps[:, n % 4, 0:4 * rows].rearrange("p (k r) -> p k r", k=4)).then_inc(x_evd, 1)
            for g in range(NG):
                dve.wait_ge(bias_mm, g + 1)
                dve.tensor_copy(rvec[:, g, :], ps[0:HG, 4 + g, 0:384]).then_inc(bias_ev, 1)
            dve.wait_ge(bias_mm, 4)
            dve.tensor_copy(sbias[:], ps[:, 4, 0:96]).then_inc(acc_free, 1)
            dve.tensor_copy(nbias[:], ps[0:NS, 5, 0:96]).then_inc(acc_free, 1)
            dve.wait_ge(cols_ok, 1)
            rms(0)
            for k in range(2):
                split_lo(k, 0, k)
            dve.wait_ge(x_evd, 6)
            dve.wait_ge(x_eva, 6)
            norm_split(0, xT0, 0, 0)
            dve.wait_ge(wf_h, 1)
            dve.tensor_tensor(wf_lo[:], wf[:], wf_hi[:].bitcast(F32), ALU.subtract).then_inc(wf_l, 1)

            z, a, e, s1, s2, p = (lfw[:, n, :] for n in range(6))
            link(dve.memset(lfw[:, 0, :], 0.0))
            dve.wait_ge(f_mm, 1)
            dve.tensor_tensor(z[:, 0:16].rearrange("p (t h) -> p t h", t=2), ps[:, 6, 0:16].rearrange("p (t h) -> p t h", t=2),
                              bfb[:].unsqueeze(1).broadcast_to([P, 2, 8]), ALU.add)
            link(dve.tensor_tensor(z[0:NS, 16:24], ps[0:NS, 6, 16:24], bfb[0:NS, :], ALU.add))
            dve.scalar_tensor_tensor(out=a, in0=z, scalar=-1.0, in1=z, op0=ALU.mult, op1=ALU.max).then_inc(lf_z, 1)
            dve.wait_ge(lf_exp, 1)
            link(dve.tensor_scalar(s1, e, 2.0, None, ALU.add))
            link(dve.reciprocal(s1, s1))
            link(dve.tensor_tensor(s1, s1, e, ALU.mult))
            link(dve.tensor_tensor(s2, s1, s1, ALU.mult))
            link(dve.tensor_scalar(p, s2, 1.0 / 15, None, ALU.mult))
            for n in (13, 11, 9, 7, 5, 3):
                link(dve.scalar_tensor_tensor(out=p, in0=p, scalar=1.0 / n, in1=s2, op0=ALU.add, op1=ALU.mult))
            link(dve.scalar_tensor_tensor(out=p, in0=p, scalar=1.0, in1=s1, op0=ALU.add, op1=ALU.mult))
            link(dve.tensor_scalar(z, z, 0.0, None, ALU.min))
            dve.scalar_tensor_tensor(out=lf[:].rearrange("p t h -> p (t h)"), in0=p, scalar=-2.0, in1=z,
                                     op0=ALU.mult, op1=ALU.add).then_inc(lf_ok, 1)

            def qkv(u0, kv0, n):
                trips = n // 4
                for kind in "qkv":
                    base = u0 + n * "qkv".index(kind)
                    with dve.Fori(0, trips) as i:
                        for k in range(4):
                            h = i * 4 + k
                            step(i * 4 + (base + k), k)
                            out = ps[:, k, 0:T]
                            if kind == "q":
                                dve.tensor_scalar(pT[:, bass.ds(h, 1), :].rearrange("p o n -> p (o n)"), out[:, 0:SEQ], SCALE, None, ALU.mult)
                                dve.tensor_scalar(sT[:, bass.ds(h + s_at, 1), :].rearrange("p o n -> p (o n)"), out[:, SEQ:T], SCALE, None,
                                                  ALU.mult).then_inc(acc_free, 1)
                                continue
                            kv = i * 4 + (kv0 + n * (kind == "v") + k)
                            dve.wait_ge(nat_t, kv + 1)
                            if kind == "k":
                                dve.tensor_copy(pT[:, bass.ds(h + n, 1), :].rearrange("p o n -> p (o n)"), out[:, 0:SEQ])
                                dve.tensor_copy(sT[:, bass.ds(h + s_at + NQ, 1), :].rearrange("p o n -> p (o n)"), out[:, SEQ:T])
                            dve.tensor_copy(v_stage[:, k % 2, :], out).then_inc(acc_free, 1)

            s_at = 0
            dve.wait_ge(xT_spill, 16)
            dve.wait_ge(rvec_st, 16)
            qkv(U_FQ, 0, HF)

            dve.wait_ge(k_out[0], 64)
            dve.wait_ge(k_out[1], 64)
            dve.wait_ge(nat_t, 18)
            dve.memset(negones[:], -1.0)
            dve.wait_ge(pa_cum, 2)
            dve.tensor_copy(gkeep[:], ps[0:NS, 7, 0:8])
            link(dve.tensor_copy(cTs[:], ps[0:8, 6, 0:SEQ]))
            dve.tensor_tensor(cTd[:], cTs[:].unsqueeze(1).broadcast_to([8, HF, SEQ]),
                              ident[0:8, 0:8].unsqueeze(2).broadcast_to([8, HF, SEQ]), ALU.mult).then_inc(pa_pre, 1)
            dve.wait_ge(pa_pre, 1)
            dve.engine_nop().then_inc(pa_free, 1)

            def normalise(parts, per_key):
                link(dve.reciprocal(stat[:, 4:6], stat[:, 2:4]))
                for n, x in enumerate(parts):
                    dve.tensor_scalar(x, x, stat[:, 4 + n:5 + n], None, ALU.mult).then_inc(per_key, 1)

            def out_parts(h, src, done):
                hi = o_hi[:, bass.ds(h, 1), 0:SEQ].rearrange("p o n -> p (o n)")
                lo = o_lo[:, bass.ds(h, 1), 0:SEQ].rearrange("p o n -> p (o n)")
                link(dve.tensor_copy(hi, src))
                dve.tensor_tensor(lo, src, hi.bitcast(F32), ALU.subtract).then_inc(done, 1)

            with dve.Fori(0, HF) as h:
                ch.enter(h, 2)
                dve.wait_ge(pa_s, h + 1)
                dve.tensor_reduce(stat[:, 0:1], ps[:, 0, 0:P], AX, ALU.max, negate=True).then_inc(pa_m, 1)
                dve.tensor_reduce(stat[:, 1:2], ps[:, 0, P:384], AX, ALU.max, negate=True).then_inc(pa_m, 1)
                dve.wait_ge(pa_e, h * 2 + 2)
                normalise((pr[:, 0, 0:P], pr[:, 0, P:384]), pa_p)
                dve.wait_ge(pa_o, h + 1)
                out_parts(h, ps[:, 3, 0:SEQ], pa_free)
            ch.leave(HF)

            s_at = HF
            qkv(U_DQ, 16, HDIL)

            dve.engine_nop().then_inc(pd_free, 1)
            with dve.Fori(0, HG) as h:
                ch.enter(h, 2)
                dve.wait_ge(pd_s, h + 1)
                for n, part in enumerate((slice(0, P), slice(P, 384))):
                    dve.tensor_reduce(stat[:, n:n + 1], ps[:, 0:NG, part], mybir.AxisListType.XY, ALU.max, negate=True).then_inc(pd_m, 1)
                dve.wait_ge(pd_e, h * 2 + 2)
                normalise((pr[:, :, 0:P], pr[:, :, P:384]), pd_p)
                dve.wait_ge(pd_o, h * NG + NG)
                out_parts(h + HF, ps[:, 6, 0:SEQ], pd_free)
            ch.leave(HG)

            dve.wait_ge(lft_t, 1)
            for n in range(2):
                ins = dve.tensor_copy(lft[:, 4 * n:4 * n + 4].rearrange("p h b g -> p (h b g)"), ps[:, n, :])
            ins.then_inc(lft_ok, 1)
            dve.wait_ge(lft_ok, 1)
            link(dve.memset(lfs[:, :, :, NPG - 1:NPG], 0.0))
            for g in range(NPG - 2, -1, -1):
                link(dve.tensor_tensor(lfs[:, :, :, g:g + 1], lfs[:, :, :, g + 1:g + 2], lft[:, :, :, g + 1:g + 2], ALU.add))
            dve.engine_nop().then_inc(lfs_ok, 1)
            dve.wait_ge(sn_mm, 1)
            grid = "p (h c) -> p h c"
            dve.tensor_tensor(sn[:, 0:HF, :], ps[0:NS, 4, :].rearrange(grid, h=HF),
                              gkeep[:].unsqueeze(2).broadcast_to([NS, HF, NS]), ALU.subtract)
            for h0, n, bank in ((0, 8, 5), (8, 4, 6)):
                bias = nbias[:, 8 * h0:8 * h0 + 8 * n].rearrange("p (h q) -> p h q", q=DT)
                ins = dve.tensor_tensor(sn[:, HF + h0:HF + h0 + n, :].rearrange("p h (b q) -> p h b q", b=DB),
                                        ps[0:NS, bank, 0:64 * n].rearrange("p (h b q) -> p h b q", h=n, b=DB),
                                        bias.unsqueeze(2).broadcast_to([NS, n, DB, DT]), ALU.add)
            link(ins)
            link(dve.tensor_tensor(sn[:], sn[:], blk[:].unsqueeze(1).broadcast_to([NS, NQ, NS]), ALU.add))
            dve.wait_ge(bk_mm, 1)
            for n in range(2):
                ins = dve.tensor_copy(bk[:, 4 * n:4 * n + 4].rearrange("p h b g -> p (h b g)"), ps[:, 2 + n, :])
            ins.then_inc(pre_ok, 1)
            dve.wait_ge(pre_ok, 1)

            def queries(b):
                wait_pos(dve, sc_done, b * KPG)
                dve.tensor_copy(qb[:], sT[:, 0:NQ, bass.ds(b * DT, DT)]).then_inc(qb_ok, 1)

            def keys_b(b, s):
                dve.wait_ge(tr_b, n_b(b, s) + 1)
                wait_pos(dve, sc_done, b * KPG + (s - kt_back(s) + 1))
                dve.tensor_copy(kT[:, s % 2, 512:1024], ps[:, 3, :]).then_inc(kt_b, 1)

            def take_out(b):
                dve.wait_ge(o_done, b + 1)
                link(dve.tensor_tensor(ot[:], ps[:, 7, 0:96], rl[:], ALU.mult))
                x = ot[:].rearrange("p (h q) -> p h q", q=DT)
                hi = o_hi[:, :, bass.ds(b * DT + SEQ, DT)]
                lo = o_lo[:, :, bass.ds(b * DT + SEQ, DT)]
                link(dve.tensor_copy(hi, x))
                dve.tensor_tensor(lo, x, hi.bitcast(F32), ALU.subtract).then_inc(o_ev, 1)

            def gate_out(g, k):
                wait_pos(dve, g_st, g * 16)
                dve.tensor_scalar(g_stage[:], ps[:, k % 2, 0:T], cols[:, bass.ds(g + 64, 1)], None, ALU.add).then_inc(acc_free, 1)

            hq = "p (h q) -> p h q"

            def sequence(b):
                queries(b)
                for s in range(KPG):
                    if s != NPG:
                        keys_b(b, s)
                if not isinstance(b, int):
                    take_out(b - 1)
                dve.wait_ge(sc_done, b * KPG + KPG)
                for n in range(2):
                    dve.tensor_tensor(pf[:, 8 * n:8 * n + 8], ps[:, 4 + n, :].rearrange("p (g h q) -> p g h q", g=8, h=HF),
                                      bk[:, :, bass.ds(b, 1), 8 * n:8 * n + 8].rearrange("p h o g -> p (o g) h").unsqueeze(3).broadcast_to([P, 8, HF, DT]),
                                      ALU.add)
                link(dve.tensor_tensor(pd[:], ps[:, 6, 0:96], sbias[:], ALU.add))
                dve.tensor_reduce(m1[:, 0:64], pf[:].rearrange("p g h q -> p (h q) g"), AX, ALU.max).then_inc(s_read, 1)
                dve.tensor_reduce(m1[:, 64:96], pd[:].rearrange("p (g c) -> p c g", g=NG), AX, ALU.max)
                new = sn[:, :, bass.ds(b * DT, DT)]
                link(dve.tensor_reduce(nm[:].rearrange(hq, q=DT), new[:, HF:NQ, :].rearrange("p (g h) q -> p h q g", g=NG), AX, ALU.max))
                dve.tensor_tensor(m1[0:NS, 0:64].rearrange(hq, q=DT), m1[0:NS, 0:64].rearrange(hq, q=DT), new[:, 0:HF, :], ALU.max)
                dve.tensor_tensor(m1[0:NS, 64:96], m1[0:NS, 64:96], nm[:], ALU.max).then_inc(m1_ok, 1)
                g = b * 4
                step(g + U_GATE, 0)
                gate_out(g, 0)
                dve.wait_ge(mt_ok, b + 1)
                link(dve.tensor_reduce(mx[:], ps[0:96, 6, 0:P], AX, ALU.max))
                dve.tensor_scalar(dg[:], ident[0:96, 0:96], mx[:], None, ALU.mult).then_inc(dg_ok, 1)
                step(g + (U_GATE + 1), 1)
                gate_out(g + 1, 1)
                dve.wait_ge(mb_mm, b + 1)
                link(dve.tensor_copy(mb[:], ps[:, 6, P:P + 96]))
                dve.tensor_tensor(pf[:].rearrange("p g h q -> p g (h q)"), pf[:].rearrange("p g h q -> p g (h q)"),
                                  mb[:, 0:64].unsqueeze(1).broadcast_to([P, NPG, 64]), ALU.subtract)
                dve.tensor_tensor(pd[:].rearrange("p (g c) -> p g c", g=NG), pd[:].rearrange("p (g c) -> p g c", g=NG),
                                  mb[:, 64:96].unsqueeze(1).broadcast_to([P, NG, 32]), ALU.subtract)
                dve.tensor_tensor(pn[:, 0:HF, :], new[:, 0:HF, :], mb[0:NS, 0:64].rearrange(hq, q=DT), ALU.subtract)
                dve.tensor_tensor(pn[:, HF:NQ, :].rearrange("p (g h) q -> p g h q", g=NG), new[:, HF:NQ, :].rearrange("p (g h) q -> p g h q", g=NG),
                                  mb[0:NS, 64:96].rearrange(hq, q=DT).unsqueeze(1).broadcast_to([NS, NG, HG, DT]), ALU.subtract).then_inc(sub_ok, 1)
                dve.wait_ge(p_ok, b * 3 + 3)
                dve.tensor_reduce(m1[:, 0:64], pf[:].rearrange("p g h q -> p (h q) g"), AX, ALU.add)
                dve.tensor_reduce(m1[:, 64:96], pd[:].rearrange("p (g c) -> p c g", g=NG), AX, ALU.add)
                link(dve.tensor_reduce(nm[:].rearrange(hq, q=DT), pn[:, HF:NQ, :].rearrange("p (g h) q -> p h q g", g=NG), AX, ALU.add))
                dve.tensor_tensor(m1[0:NS, 0:64].rearrange(hq, q=DT), m1[0:NS, 0:64].rearrange(hq, q=DT), pn[:, 0:HF, :], ALU.add)
                dve.tensor_tensor(m1[0:NS, 64:96], m1[0:NS, 64:96], nm[:], ALU.add).then_inc(l1_ok, 1)
                step(g + (U_GATE + 2), 2)
                gate_out(g + 2, 2)
                dve.wait_ge(sum_mm, b + 1)
                dve.reciprocal(rl[:], ps[:, 6, 256:352]).then_inc(rl_ok, 1)
                step(g + (U_GATE + 3), 3)
                gate_out(g + 3, 3)

            sequence(0)
            with dve.Fori(1, DB) as b:
                ch.enter(b - 1, 7)
                sequence(b)
            ch.leave(DB - 1)
            dve.wait_ge(rl_ok, DB)
            take_out(DB - 1)

            dve.wait_ge(g_sig, 4)
            with dve.Fori(0, KT // 4) as i:
                ch.enter(i, 12)
                for k in range(4):
                    e1 = i * 4 + k
                    step(i * 4 + (U_O + k), k)
                    a1, a2 = mtmp[:, k % 2, 0, :], mtmp[:, k % 2, 1, :]
                    one = lambda x, n: x[:, bass.ds(n, 1), :].rearrange("p o n -> p (o n)")
                    dve.tensor_tensor(a1, ps[:, k, 0:T], one(gates, e1), ALU.mult)
                    link(dve.tensor_tensor(a2, ps[:, 4 + k, 0:T], one(gates, e1 + KT), ALU.mult))
                    link(dve.tensor_tensor(a1, a1, a2, ALU.add))
                    link(dve.tensor_copy(one(act_hi, e1), a1))
                    dve.tensor_tensor(one(act_lo, e1), a1, one(act_hi, e1).bitcast(F32), ALU.subtract).then_inc(acc_free, 1)
            ch.leave(KT // 4)
            with dve.Fori(0, KT // 4) as i:
                for k in range(4):
                    step(i * 4 + (U_OUT + k), k)
                    dve.tensor_copy(outT[:, bass.ds(i * 4 + k, 1), :].rearrange("p o n -> p (o n)"), ps[:, k, 0:T]).then_inc(acc_free, 1)

            def add_normed(n, src, c, dst):
                rms(n)
                for k in range(KT):
                    ins = normed(src[:, k, :], src[:, k, :], c, k)
                link(ins)
                for q in range(4):
                    b4 = slice(4 * q, 4 * q + 4)
                    dve.tensor_tensor(dst[:, b4, :], dst[:, b4, :], src[:, b4, :], ALU.add).then_inc(nrm_done, 1)
                dve.wait_ge(nrm_done, 4 * n + 4)

            dve.wait_ge(xT_ld, 16)
            add_normed(1, outT, 16, xT)
            rms(2)
            norm_split(4, xT, 32, 8)

            dve.wait_ge(x1_st, 16)
            with dve.Fori(0, FB // 2) as i:
                for k in range(4):
                    step(i * 4 + (U_UP + k), k)
                    if k < 2:
                        dve.wait_ge(sg_done, i * 2 + (k + 1))
                        dve.tensor_tensor(gs[:, k, :], ps[:, k, 0:T], sig[:, k, :], ALU.mult).then_inc(acc_free, 1)
                    else:
                        dve.wait_ge(acc_free, i * 4 + (U_UP + k + 1))
                        dve.tensor_tensor(hid[:, bass.ds(i * 2 + (k - 2), 1), :].rearrange("p o n -> p (o n)"),
                                          ps[:, k, 0:T], gs[:, k - 2, :], ALU.mult).then_inc(acc_free, 1)

            def quarter_lo(kq):
                hi, lo = (a_hi, a_lo) if kq % 2 else (q_hi, q_lo)
                dve.wait_ge(q_h, kq + 1)
                dve.tensor_tensor(lo[:], hid[:, KQ * kq:KQ * kq + KQ, :], hi[:].bitcast(F32), ALU.subtract).then_inc(q_l, 1)

            def down_out(u, kq, e, k):
                dst = yacc[:, bass.ds(e, 1), :].rearrange("p o n -> p (o n)")
                if kq == 0:
                    dve.tensor_copy(dst, ps[:, k, 0:T]).then_inc(acc_free, 1)
                else:
                    dve.tensor_tensor(dst, dst, ps[:, k, 0:T], ALU.add).then_inc(acc_free, 1)

            dve.wait_ge(acc_free, U_DOWN + 2)
            quarter_lo(0)
            for kq in range(4):
                u0 = U_DOWN + 16 * kq

                def down_trips(a, b):
                    with dve.Fori(a, b) as i:
                        for k in range(4):
                            step(i * 4 + (u0 + k), k, KQ)
                            down_out(None, kq, i * 4 + k, k)

                down_trips(0, 2)
                if kq < 3:
                    quarter_lo(kq + 1)
                    down_trips(2, 4)
                else:
                    for k in range(8):
                        if k < 6:
                            step(u0 + 8 + k, k % 4, KQ)
                        else:
                            dve.wait_ge(unit_done, u0 + 9 + k)
                        down_out(None, kq, 8 + k, k % 4)

            dve.wait_ge(acc_free, U_END + 2)
            dve.wait_ge(x1_ld, 16)
            add_normed(3, yacc, 48, x1T)
            for n in range(0, 12, 2):
                t, q = divmod(n, 4)
                rows = P if t < 2 else NS
                dve.wait_ge(y_tr, n + 1)
                dve.tensor_copy(y_nat[0:rows, t, 512 * q:512 * q + 512], ps[0:rows, n % 4, :]).then_inc(y_evd, 1)


_INS = ['x_prompt', 'x_sample', 'cache_fox_k', 'cache_fox_v', 'cache_fox_logf', 'page_table',
        'cache_win1_k', 'cache_win1_v', 'cache_win2_k', 'cache_win2_v', 'cache_win3_k', 'cache_win3_v',
        'rel_bias_table', 'norm_pre_mix', 'norm_post_mix', 'norm_pre_ffn', 'norm_post_ffn',
        'w_in', 'b_forget', 'w_gate', 'b_gate', 'w_o_fox', 'w_o_dil', 'w_out', 'w_gate_up', 'w_down']
_OUTS = ([('y_prompt', (1, SEQ, DM)), ('y_sample', (DB, DT, DM)),
          ('fox_k_prompt', (1, 1, SEQ, HF, HD)), ('fox_v_prompt', (1, 1, SEQ, HF, HD)), ('fox_logf_prompt', (1, 1, SEQ, HF)),
          ('fox_k_sample', (1, DB, DT, HF, HD)), ('fox_v_sample', (1, DB, DT, HF, HD)), ('fox_logf_sample', (1, DB, DT, HF))]
         + [(f'win{g + 1}_{x}_prompt', (1, 1, min(w, SEQ), HG, HD)) for g, (w, _) in enumerate(DIL) for x in 'kv']
         + [(f'win{g + 1}_{x}_sample', (1, DB, w, HG, HD)) for g, (w, _) in enumerate(DIL) for x in 'kv'])
_SCRATCH = {'xT': (KT, P, T), 'x1T': (KT, P, T), 'gates': (2 * KT, P, T), 'rvec': (HG, NG, 384),
            'hankel': (HG, P, NG, SEQ), 'kd': (NS, HDIL * HD), 'vd': (NS, HDIL * HD)}


def kernel(**inputs):
    import concourse.bacc as _bacc
    from concourse.bass_utils import run_bass_kernel_spmd as _run

    nc = _bacc.Bacc("TRN2", target_bir_lowering=False, num_devices=1)
    arrays, ins, outs, scratch = {}, {}, {}, {}
    for name in _INS + ['shape_consts', 'bucket_picks']:
        a = {'shape_consts': shape_consts, 'bucket_picks': bucket_picks}[name]() if name not in inputs else inputs[name]
        a = np.ascontiguousarray(a)
        arrays[f"in_{name}"] = a
        ins[name] = nc.dram_tensor(f"in_{name}", a.shape, mybir.dt.from_np(a.dtype), kind="ExternalInput").ap()
    for name, shape in _OUTS:
        outs[name] = nc.dram_tensor(f"out_{name}", shape, F32, kind="ExternalOutput").ap()
    for name, shape in _SCRATCH.items():
        scratch[name] = nc.dram_tensor(f"scratch_{name}", shape, F32, kind="Internal").ap()
    build(nc, ins, outs, scratch)
    r = _run(nc, [arrays], core_ids=[0])
    return tuple(r.results[0][f"out_{name}"] for name, _ in _OUTS)
```
